# Optimizing a Trainium2 kernel written in Bass

```python
import jax, jax.numpy as jnp
from jax import lax
import numpy as np

D_MODEL = 1024
BATCH = 1
SEQ = 512
DEPTH = 1

HEAD_DIM = 64
SB_HEADS = 8
SA_HEADS = 8
SA_KV_HEADS = 2
IDX_HEADS = 8
IDX_DIM = 32
TOPK_MAX = 256
Q_BLOCK = 128
D_FF = 4 * D_MODEL
EPS = 1e-6

SB_W = SB_HEADS * HEAD_DIM
SA_QW = SA_HEADS * HEAD_DIM
SA_KVW = SA_KV_HEADS * HEAD_DIM
IDX_QW = IDX_HEADS * IDX_DIM
SPLIT_SIZES = (SB_W, SB_W, SB_W, SA_QW, SA_KVW, SA_KVW, IDX_QW, IDX_DIM, IDX_HEADS, D_MODEL, D_MODEL)
PROJ_W = SB_W * 3 + SA_QW + 2 * SA_KVW + IDX_QW + IDX_DIM + IDX_HEADS + 2 * D_MODEL

kernel_name = "hybrid_stickbreak_dsa_gated_block"

def _rmsnorm(x, g):
    xf = x.astype(jnp.float32)
    xf = xf * lax.rsqrt(jnp.mean(xf * xf, axis=-1, keepdims=True) + EPS)
    return (xf * g.astype(jnp.float32)).astype(x.dtype)

def _split_cols(p):
    offs = np.cumsum(SPLIT_SIZES)[:-1].tolist()
    return jnp.split(p, offs, axis=-1)

def _stick_breaking(q, k, v):
    B, S, H, D = q.shape
    nblk = S // Q_BLOCK
    scale = D ** -0.5
    key_pos = jnp.arange(S)

    def block(i):
        qb = lax.dynamic_slice_in_dim(q, i * Q_BLOCK, Q_BLOCK, axis=1)
        z = jnp.einsum('bthd,bshd->bhts', qb, k,
                       preferred_element_type=jnp.float32) * scale
        qpos = i * Q_BLOCK + jnp.arange(Q_BLOCK)
        causal = key_pos[None, :] < qpos[:, None]
        log_beta = jax.nn.log_sigmoid(z)
        log_1mb = jnp.where(causal, jax.nn.log_sigmoid(-z), 0.0)
        later = lax.cumsum(log_1mb, axis=3, reverse=True) - log_1mb
        attn = jnp.where(causal, jnp.exp(log_beta + later), 0.0)
        return jnp.einsum('bhts,bshd->bthd', attn.astype(v.dtype), v)

    out = lax.map(block, jnp.arange(nblk))
    return out.transpose(1, 0, 2, 3, 4).reshape(B, S, H * D)

def _gather_rows(a, idx):
    return jax.vmap(lambda ab, ib: ab[ib])(a, idx)

def _dsa_attention(q, k, v, q_idx, k_idx, w_idx, slopes, top_k):
    B, S, Hq, D = q.shape
    Hkv = k.shape[2]
    G = Hq // Hkv
    Hi, Di = q_idx.shape[2], q_idx.shape[3]
    nblk = S // Q_BLOCK
    key_pos = jnp.arange(S)
    slopes_g = slopes.reshape(Hkv, G)

    def block(i):
        start = i * Q_BLOCK
        qpos = start + jnp.arange(Q_BLOCK)
        qb = lax.dynamic_slice_in_dim(q, start, Q_BLOCK, axis=1)
        qib = lax.dynamic_slice_in_dim(q_idx, start, Q_BLOCK, axis=1)
        wb = lax.dynamic_slice_in_dim(w_idx, start, Q_BLOCK, axis=1)
        rel = jnp.einsum('bthd,bsd->bths', qib, k_idx,
                         preferred_element_type=jnp.float32) * (Di ** -0.5)
        score = jnp.einsum('bth,bths->bts', wb.astype(jnp.float32), jax.nn.relu(rel))
        score = jnp.where(key_pos[None, None, :] <= qpos[None, :, None], score, -jnp.inf)
        _, idx = lax.top_k(score, top_k)
        valid = idx <= qpos[None, :, None]
        k_sel = _gather_rows(k, idx)
        v_sel = _gather_rows(v, idx)
        qg = qb.reshape(B, Q_BLOCK, Hkv, G, D)
        s = jnp.einsum('btgrd,btkgd->btgrk', qg, k_sel,
                       preferred_element_type=jnp.float32) * (D ** -0.5)
        dist = (qpos[None, :, None] - idx).astype(jnp.float32)
        s = s - slopes_g[None, None, :, :, None] * dist[:, :, None, None, :]
        s = jnp.where(valid[:, :, None, None, :], s, -jnp.inf)
        p = jax.nn.softmax(s, axis=-1)
        o = jnp.einsum('btgrk,btkgd->btgrd', p.astype(v.dtype), v_sel)
        return o.reshape(B, Q_BLOCK, Hq * D)

    out = lax.map(block, jnp.arange(nblk))
    return out.transpose(1, 0, 2, 3).reshape(B, S, Hq * D)

def setup_inputs(seed: int = 0) -> dict:
    key = jax.random.key(seed)
    ks = jax.random.split(key, 16)
    L = DEPTH

    def nrm(k, shape, fan_in):
        return jax.random.normal(k, shape, jnp.float32) * (fan_in ** -0.5)

    def gain(k, shape):
        return 1.0 + 0.02 * jax.random.normal(k, shape, jnp.float32)

    return {
        "x": jax.random.normal(ks[0], (BATCH, SEQ, D_MODEL), jnp.float32),
        "norm_mix": gain(ks[1], (L, D_MODEL)),
        "w_in": nrm(ks[2], (L, D_MODEL, PROJ_W), D_MODEL),
        "q_norm_sb": gain(ks[3], (L, HEAD_DIM)),
        "k_norm_sb": gain(ks[4], (L, HEAD_DIM)),
        "q_norm_sa": gain(ks[5], (L, HEAD_DIM)),
        "k_norm_sa": gain(ks[6], (L, HEAD_DIM)),
        "w_branch_sb": nrm(ks[7], (L, SB_W, D_MODEL), SB_W),
        "w_branch_sa": nrm(ks[8], (L, SA_QW, D_MODEL), SA_QW),
        "w_out": nrm(ks[9], (L, D_MODEL, D_MODEL), D_MODEL),
        "norm_mlp": gain(ks[10], (L, D_MODEL)),
        "w_ff1": nrm(ks[11], (L, D_MODEL, D_FF), D_MODEL),
        "w_ff2": nrm(ks[12], (L, D_FF, D_MODEL), D_FF),
    }

def reference(x, norm_mix, w_in, q_norm_sb, k_norm_sb, q_norm_sa, k_norm_sa,
              w_branch_sb, w_branch_sa, w_out, norm_mlp, w_ff1, w_ff2):
    B, S, _ = x.shape
    top_k = min(TOPK_MAX, S // 4)
    slopes = jnp.exp2(-8.0 * jnp.arange(1, SA_HEADS + 1, dtype=jnp.float32) / SA_HEADS)

    for l in range(DEPTH):
        h = _rmsnorm(x, norm_mix[l])
        proj = h @ w_in[l]
        (q_sb, k_sb, v_sb, q_sa, k_sa, v_sa,
         q_ix, k_ix, w_ix, g_sb, g_sa) = _split_cols(proj)

        q_sb = _rmsnorm(q_sb.reshape(B, S, SB_HEADS, HEAD_DIM), q_norm_sb[l])
        k_sb = _rmsnorm(k_sb.reshape(B, S, SB_HEADS, HEAD_DIM), k_norm_sb[l])
        v_sb = v_sb.reshape(B, S, SB_HEADS, HEAD_DIM)
        o_sb = _stick_breaking(q_sb, k_sb, v_sb)

        q_sa = _rmsnorm(q_sa.reshape(B, S, SA_HEADS, HEAD_DIM), q_norm_sa[l])
        k_sa = _rmsnorm(k_sa.reshape(B, S, SA_KV_HEADS, HEAD_DIM), k_norm_sa[l])
        v_sa = v_sa.reshape(B, S, SA_KV_HEADS, HEAD_DIM)
        q_ix = q_ix.reshape(B, S, IDX_HEADS, IDX_DIM)
        w_ix = w_ix * (IDX_HEADS ** -0.5)
        o_sa = _dsa_attention(q_sa, k_sa, v_sa, q_ix, k_ix, w_ix, slopes, top_k)

        merged = (jax.nn.sigmoid(g_sb) * (o_sb @ w_branch_sb[l])
                  + jax.nn.sigmoid(g_sa) * (o_sa @ w_branch_sa[l]))
        x = x + merged @ w_out[l]

        h2 = _rmsnorm(x, norm_mlp[l])
        x = x + jnp.square(jax.nn.relu(h2 @ w_ff1[l])) @ w_ff2[l]

    return x


_drawn_inputs = setup_inputs


def setup_inputs(seed=0):
    import zlib

    import numpy as np

    out = dict(_drawn_inputs(seed))
    spreads = {}
    factors = {'q_norm_sb': 8.0, 'k_norm_sb': 8.0, 'q_norm_sa': 8.0, 'k_norm_sa': 8.0, 'norm_mlp': 3.367}
    for name, (base, spread) in spreads.items():
        noise = np.random.default_rng([zlib.crc32(name.encode()), seed]).standard_normal(out[name].shape)
        drawn = base * np.exp(spread * noise) if base else spread * noise
        out[name] = __import__('jax').numpy.asarray(drawn.astype(out[name].dtype))
    for name, factor in factors.items():
        out[name] = (out[name] * factor).astype(out[name].dtype)
    return out
```

```python
from contextlib import ExitStack

import concourse.bass as bass
from concourse import mybir

ALU = mybir.AluOpType
ACT = mybir.ActivationFunctionType
AX = mybir.AxisListType
F32 = mybir.dt.float32
F32R = mybir.dt.float32r
I32 = mybir.dt.int32

P = 128
S = 512
D = 1024
FF = 4 * D
TB = S // P
KD = D // P
HD = 64
SBH = 8
SAH, SAKV = 8, 2
GQ = SAH // SAKV
IXH, IXD = 8, 32
TOPK = min(256, S // 4)
EPS = 1e-6
MASKED = -1e30
TAKEN = -3e38

C_QSB, C_KSB, C_VSB, C_QSA, C_KVI = 0, 512, 1024, 1536, 2048
C_KW = 2560
C_GATE = 2600

RAW, CUT, SLAB = 4, 2, 2048

GROUPS = [C_KVI, C_QSB, C_KSB, C_QSA, C_VSB]
KVI, QSB, KSB, QSA, VSB = range(5)
SL_PROJ = 0
SL_GATE = SL_PROJ + 2 * len(GROUPS)
SL_BR = SL_GATE + 8
SL_OUT = SL_BR + 4
SL_FF = SL_OUT + 4
FG = 4
SL_END = SL_FF + 8 * FG

ZCOL = [0, 512, 1024, 896]
ZW = 1280


def block_kernel(nc, x, norm_mix, w_in, q_norm_sb, k_norm_sb, q_norm_sa, k_norm_sa,
                 w_branch_sb, w_branch_sa, w_out, norm_mlp, w_ff1, w_ff2, out):
    ctx = ExitStack()
    with ctx:
        def sb(name, shape, dt, where=ctx):
            return where.enter_context(nc.sbuf_tensor(name, shape, dt))

        def sem(name):
            return ctx.enter_context(nc.semaphore(name))

        raw = sb("raw", [P, RAW, SLAB], F32)
        cut_hi = sb("cut_hi", [P, CUT, SLAB], F32R)
        cut_lo = sb("cut_lo", [P, CUT, SLAB], F32R)
        a_hi = sb("a_hi", [P, KD, S], F32R)
        a_lo = sb("a_lo", [P, KD, S], F32R)
        gates = sb("gates", [P, 16, S], F32)
        qT_sb = sb("qT_sb", [P, 4, S], F32)
        qT_sa = sb("qT_sa", [P, 4, S], F32)
        ident = sb("ident", [P, P], F32)
        const_f = sb("const_f", [P, 3, P], F32)
        const_r = sb("const_r", [P, 4, P], F32R)
        ident_r, tri_r, ones_r, mask_r = (const_r[:, j, :] for j in range(4))
        dist = sb("dist", [P, S], F32)
        dist_i = dist[:, :].bitcast(I32)
        gain_rows = sb("gain_rows", [20, P], F32)
        gain = sb("gain", [P, 20], F32)
        kw_raw = sb("kw_raw", [P, KD, 40], F32)
        kw_hi = sb("kw_hi", [P, KD, 40], F32R)
        kw_lo = sb("kw_lo", [P, KD, 40], F32R)
        w_tok = sb("w_tok", [P, TB, IXH], F32)
        row_ss = sb("row_ss", [P, 2 * TB], F32)
        row_ms = sb("row_ms", [P, 2 * TB], F32)
        row_r = sb("row_r", [P, 2 * TB], F32)
        head_ss = sb("head_ss", [P, 2, 8], F32)
        head_ms = sb("head_ms", [P, 2, 8], F32)
        head_r = sb("head_r", [P, 2, 8], F32)
        minus_half = sb("minus_half", [P, 8], F32)
        best8 = sb("best8", [P, 8], F32)
        smax = sb("smax", [P, 2], F32)
        snmax = sb("snmax", [P, 2], F32)
        psum_l = sb("psum_l", [P, 2], F32)
        rcp_l = sb("rcp_l", [P, 2], F32)

        early = ExitStack()
        kv_sb = sb("kv_sb", [P, 2, 4, S], F32, early)
        kT_sb, v_sb = kv_sb[:, 0], kv_sb[:, 1]
        kT_sa = sb("kT_sa", [P, S], F32, early)
        v_sa = sb("v_sa", [P, TB, P], F32, early)
        lg = sb("lg", [P, 2, ZW], F32, early)
        sp_hi = sb("sp_hi", [P, ZW], F32R, early)
        sp_lo = sb("sp_lo", [P, ZW], F32R, early)
        topm = sb("topm", [P, ZW], F32, early)
        early.close()
        late = ExitStack()
        b_hi = sb("b_hi", [P, KD, S], F32R, late)
        b_lo = sb("b_lo", [P, KD, S], F32R, late)
        xres = sb("xres", [P, TB, D], F32, late)
        late.close()

        def slot(j, n=1):
            return gates[:, j:j + n, :].rearrange("p a b -> p (a b)")
        x_tok = gates[:, 0:8, :].rearrange("p (m a) b -> p m (a b)", m=TB)
        SQ = 8
        TMP = 10
        tok = [slot(0), slot(1)]
        qixT = [slot(3), slot(4)]
        kixT, kw_sb = slot(5), slot(6)
        rel = [slot(7), slot(8)]
        MOFF = [0, 128, 384, 768]
        topmask = [topm[:, MOFF[b]:MOFF[b] + (b + 1) * P] for b in range(TB)]
        sa_s = [lg[:, 0, 0:S], lg[:, 0, S:2 * S]]
        sa_bias = [lg[:, 1, 0:S], lg[:, 1, S:2 * S]]
        pT = [kv_sb[:, j] for j in range(2)]

        ps = ctx.enter_context(nc.psum_tensor("ps", [P, 8 * S], F32))

        def bank(j, a=0, b=S):
            return ps[:, j * S + a:j * S + b]

        x_in = [sem(f"x_in{m}") for m in range(TB)]
        x2_in = sem("x2_in")
        gains_in, kw_in = sem("gains_in"), sem("kw_in")
        raw_in = [sem(f"raw_in{j}") for j in range(RAW)]
        hi_done, lo_done, half_done = sem("hi_done"), sem("lo_done"), sem("half_done")
        pool_self, dve_self, act_self = sem("pool_self"), sem("dve_self"), sem("act_self")
        ident_done, const_made, const_cut, dist_done = sem("ident_done"), sem("const_made"), sem("const_cut"), sem("dist_done")
        gain_t, gain_ready = sem("gain_t"), sem("gain_ready")
        kw_hi_done, kw_cut = sem("kw_hi_done"), sem("kw_cut")
        row_sq, row_ready, row_scaled = sem("row_sq"), sem("row_ready"), sem("row_scaled")
        nt_done, nt_gained, nt_hi, nt_cut = sem("nt_done"), sem("nt_gained"), sem("nt_hi"), sem("nt_cut")
        proj_done, sq_done, ss_done, hr_done = sem("proj_done"), sem("sq_done"), sem("ss_done"), sem("hr_done")
        proj_out, tr_done, tr_out = sem("proj_out"), sem("tr_done"), sem("tr_out")
        kix_done, kix_out, kix_rep, wT_done, w_ready = sem("kix_done"), sem("kix_out"), sem("kix_rep"), sem("wT_done"), sem("w_ready")
        rel_done, relu_done, score_done, causal_done, mask_ready = sem("rel_done"), sem("relu_done"), sem("score_done"), sem("causal_done"), sem("mask_ready")
        mask0 = sem("mask0")
        z_done, ln_done, sp_done, tri_done, a_done, av_done, osb_out = (sem(n) for n in (
            "z_done", "ln_done", "sp_done", "tri_done", "a_done", "av_done", "osb_out"))
        gate_done, gate_exp, gate_p1, gate_ready = (sem(n) for n in ("gate_done", "gate_exp", "gate_p1", "gate_ready"))
        bias_done, s_done, smax_done, snmax_done, p_done, pn_done, pt_done, pt_out, pv_done, osa_out = (
            sem(n) for n in ("bias_done", "s_done", "smax_done", "snmax_done", "p_done", "pn_done",
                             "pt_done", "pt_out", "pv_done", "osa_out"))
        o_hi, o_cut = sem("o_hi"), sem("o_cut")
        br_done, br_out, mg_sum, mg_hi, mg_cut = (sem(n) for n in ("br_done", "br_out", "mg_sum", "mg_hi", "mg_cut"))
        wo_done, wo_out = sem("wo_done"), sem("wo_out")
        f1_done, f1_relu, f1_sq, f1_hi, f1_cut = (sem(n) for n in ("f1_done", "f1_relu", "f1_sq", "f1_hi", "f1_cut"))
        f2_done, f2_out, y_out = sem("f2_done"), sem("f2_out"), sem("y_out")

        def rows(w, r0, nk, c0, nc_):
            return w[r0:r0 + nk * P, c0:c0 + nc_].rearrange("(k p) c -> p k c", p=P)

        x_d = x[0]
        win, wsb, wsa, wout, wf1, wf2 = w_in[0], w_branch_sb[0], w_branch_sa[0], w_out[0], w_ff1[0], w_ff2[0]

        def slab_source(i):
            if i < SL_GATE:
                g, half = divmod(i - SL_PROJ, 2)
                return [(0, P, 4, rows(win, half * 512, 4, GROUPS[g], 512))]
            if i < SL_BR:
                return [(0, P, 8, rows(win, 0, 8, C_GATE + 256 * (i - SL_GATE), 256))]
            if i < SL_OUT:
                q = i - SL_BR
                c0 = 512 * (q // 2)
                if q % 2 == 0:
                    return [(0, P, 4, rows(wsb, 0, 4, c0, 512))]
                return [(64 * g, 64, 4, wsa[256 * g:256 * g + 256, c0:c0 + 512].rearrange("(r d) c -> d r c", d=HD))
                        for g in range(SAKV)]
            if i < SL_FF:
                n, half = divmod(i - SL_OUT, 2)
                return [(0, P, 4, rows(wout, half * 512, 4, n * 512, 512))]
            g, j = divmod(i - SL_FF, 8)
            if j < 4:
                return [(0, P, 8, rows(wf1, 0, 8, 1024 * g + 256 * j, 256))]
            n, half = divmod(j - 4, 2)
            return [(0, P, 4, rows(wf2, 1024 * g + half * 512, 4, n * 512, 512))]

        def slab_arrived(i):
            n = sum(len(slab_source(j)) for j in range(i % RAW, i + 1, RAW))
            return raw_in[i % RAW], 16 * n

        def slab_used(i):
            if i < SL_GATE:
                g, half = divmod(i - SL_PROJ, 2)
                return (proj_done, 4 * g + 4) if half else (half_done, g + 1)
            if i < SL_BR:
                return gate_done, 2 * (i - SL_GATE) + 2
            if i < SL_OUT:
                return br_done, 4 * (i - SL_BR) + 4
            if i < SL_FF:
                n, half = divmod(i - SL_OUT, 2)
                return (wo_done, 4 * n + 4) if half else (half_done, len(GROUPS) + n + 1)
            g, j = divmod(i - SL_FF, 8)
            if j < 4:
                return f1_done, 8 * g + 2 * j + 2
            n, half = divmod(j - 4, 2)
            return (f2_done, 8 * g + 4 * n + 4) if half else (half_done, len(GROUPS) + 2 + 2 * g + n + 1)

        def cut_slot(i, part, k, nk):
            w = SLAB // nk
            return part[:, i % CUT, k * w:(k + 1) * w]

        def act_cut(i):
            nc.scalar.wait_ge(*slab_arrived(i))
            if i >= CUT:
                nc.scalar.wait_ge(*slab_used(i - CUT))
            nc.scalar.activation(cut_hi[:, i % CUT, :], raw[:, i % RAW, :], ACT.Copy).then_inc(hi_done, 1)

        def dve_cut(i):
            nc.vector.wait_ge(hi_done, i + 1)
            nc.vector.tensor_tensor(cut_lo[:, i % CUT, :], raw[:, i % RAW, :], cut_hi[:, i % CUT, :].bitcast(F32),
                                    ALU.subtract).then_inc(lo_done, 1)

        def stationary_weights(i, k, nk, col, dst, rhs_hi, rhs_lo, start, stop):
            w_hi = cut_slot(i, cut_hi, k, nk)[:, col:col + P]
            w_lo = cut_slot(i, cut_lo, k, nk)[:, col:col + P]
            nc.tensor.matmul(dst, w_hi, rhs_hi, start=start, stop=False)
            nc.tensor.matmul(dst, w_hi, rhs_lo, start=False, stop=False)
            return nc.tensor.matmul(dst, w_lo, rhs_hi, start=False, stop=stop)

        def moving_weights(i, k, dst, l_hi, l_lo, start, stop):
            w_hi, w_lo = cut_slot(i, cut_hi, k, 4), cut_slot(i, cut_lo, k, 4)
            nc.tensor.matmul(dst, l_hi, w_hi, start=start, stop=False)
            nc.tensor.matmul(dst, l_hi, w_lo, start=False, stop=False)
            return nc.tensor.matmul(dst, l_lo, w_hi, start=False, stop=stop)

        block = ctx.enter_context(nc.Block())

        @block.sync
        def _(sp):
            for m in range(TB):
                sp.dma_start(x_tok[:, m, :], x_d[m * P:(m + 1) * P, :]).then_inc(x_in[m], 16)
            sp.dma_start(gain_rows[0:8, :], norm_mix[0].rearrange("(a b) -> a b", b=P)).then_inc(gains_in, 16)
            sp.dma_start(gain_rows[8:16, :], norm_mlp[0].rearrange("(a b) -> a b", b=P)).then_inc(gains_in, 16)
            for j, g in enumerate((q_norm_sb, k_norm_sb, q_norm_sa, k_norm_sa)):
                for half in range(2):
                    sp.dma_start(gain_rows[16 + j:17 + j, half * HD:(half + 1) * HD], g).then_inc(gains_in, 16)

            def load(i):
                if i >= RAW:
                    sp.wait_ge(lo_done, i - RAW + 1)
                for p0, np_, nk, src in slab_source(i):
                    dst = raw[p0:p0 + np_, i % RAW, :].rearrange("p (k c) -> p k c", k=nk)
                    sp.dma_start(dst, src).then_inc(raw_in[i % RAW], 16)

            load(0)
            load(1)
            sp.dma_start(kw_raw[:, :, :], rows(win, 0, 8, C_KW, 40)).then_inc(kw_in, 16)
            for i in range(2, 6):
                load(i)
            sp.wait_ge(kix_out, 1)
            for q in range(4):
                sp.dma_start(kixT[32 * q:32 * q + 32, :], kw_sb[0:IXD, :]).then_inc(kix_rep, 16)
            for i in range(6, SL_BR + 2):
                load(i)
            sp.wait_ge(pv_done, 8)
            sp.wait_ge(pt_out, 32)
            sp.dma_start(xres[:, :, :], x_d.rearrange("(m p) c -> p m c", p=P)).then_inc(x2_in, 16)
            for i in range(SL_BR + 2, SL_END):
                load(i)
            for n in range(2):
                for m in range(TB):
                    sp.wait_ge(f2_out, 8 * (FG - 1) + 4 * n + m + 1)
                    sp.dma_start(out[0, m * P:(m + 1) * P, n * 512:(n + 1) * 512],
                                 xres[:, m, n * 512:(n + 1) * 512]).then_inc(y_out, 16)
            sp.wait_ge(y_out, 16 * 8)

        @block.gpsimd
        def _(pool):
            count = [0]

            def link(ins):
                count[0] += 1
                ins.then_inc(pool_self, 1)
                pool.wait_ge(pool_self, count[0])

            pool.memset(minus_half[:, :], -0.5)
            link(pool.memset(ident[:, :], 0.0))
            pool.affine_select(out=ident[:, :], in_=ident[:, :], compare_op=ALU.not_equal, fill=1.0, base=0,
                               pattern=[[-1, P]], channel_multiplier=1).then_inc(ident_done, 1)
            pool.memset(const_f[:, 0, :], -1.0)
            pool.memset(const_f[:, 1, :], -1.0)
            link(pool.memset(const_f[:, 2, :], 0.0))
            pool.affine_select(out=const_f[:, 0, :], in_=const_f[:, 0, :], compare_op=ALU.is_ge, fill=0.0, base=0,
                               pattern=[[-1, P]], channel_multiplier=1)
            pool.affine_select(out=const_f[:, 2, :], in_=const_f[:, 2, :], compare_op=ALU.is_gt, fill=MASKED, base=0,
                               pattern=[[1, P]], channel_multiplier=-1).then_inc(const_made, 1)
            link(pool.iota(dist_i, pattern=[[-1, S]], base=S - P, channel_multiplier=1))
            pool.tensor_copy(dist[:, :], dist_i).then_inc(dist_done, 1)
            link(pool.memset(topmask[0], 0.0))
            pool.affine_select(out=topmask[0], in_=topmask[0], compare_op=ALU.is_ge, fill=MASKED, base=0,
                               pattern=[[-1, P]], channel_multiplier=1).then_inc(mask0, 1)

            def rows_rsqrt(m):
                pool.wait_ge(row_sq, m + 1)
                link(pool.tensor_scalar(row_ms[:, m:m + 1], row_ss[:, m:m + 1], 1.0 / D, EPS, ALU.mult, ALU.add))
                pool.tensor_tensor(row_r[:, m:m + 1], row_ms[:, m:m + 1], minus_half[:, 0:1],
                                   ALU.pow).then_inc(row_ready, 1)

            for m in range(TB):
                rows_rsqrt(m)
            n_norm = 0
            for g in range(4):
                if g == QSB:
                    for b in range(1, TB):
                        pool.wait_ge(score_done, 8 * b)
                        diag = topmask[b][:, b * P:(b + 1) * P]
                        pool.affine_select(out=diag, in_=diag, compare_op=ALU.is_ge, fill=MASKED, base=0,
                                           pattern=[[-1, P]], channel_multiplier=1).then_inc(causal_done, 1)
                nh = 2 if g == KVI else 8
                for m in range(TB):
                    pool.wait_ge(ss_done, n_norm + 1)
                    j = n_norm % 2
                    link(pool.tensor_scalar(head_ms[:, j, 0:nh], head_ss[:, j, 0:nh], 1.0 / HD, EPS, ALU.mult, ALU.add))
                    pool.tensor_tensor(head_r[:, j, 0:nh], head_ms[:, j, 0:nh], minus_half[:, 0:nh],
                                       ALU.pow).then_inc(hr_done, 1)
                    n_norm += 1

            def gate_plus_one(f):
                pool.wait_ge(gate_exp, f + 1)
                pool.tensor_scalar(gates[:, f, :], gates[:, f, :], 1.0, None, ALU.add).then_inc(gate_p1, 1)

            for f in range(8):
                gate_plus_one(f)
            pool.wait_ge(dist_done, 1)
            pool.wait_ge(av_done, 8)
            pool.wait_ge(mask_ready, 3)
            for n in range(32):
                b, h = divmod(n, 8)
                w = (b + 1) * P
                if n >= 2:
                    pool.wait_ge(smax_done, n - 1)
                link(pool.tensor_scalar(sa_bias[n % 2][:, 0:w], dist[:, (3 - b) * P:S], -(2.0 ** -(h + 1)), None, ALU.mult))
                pool.tensor_tensor(sa_bias[n % 2][:, 0:w], sa_bias[n % 2][:, 0:w], topmask[b], ALU.add).then_inc(bias_done, 1)
                if n >= 6 and n % 4 == 2:
                    gate_plus_one(7 + n // 4)
            gate_plus_one(15)
            for f in range(8):
                pool.wait_ge(br_out, 8 * (f // 4) + 4 + f % 4 + 1)
                pool.tensor_tensor(gates[:, f, :], gates[:, f, :], gates[:, 8 + f, :], ALU.add).then_inc(mg_sum, 1)
            for m in range(TB):
                rows_rsqrt(TB + m)
            for c in range(FF // P):
                pool.wait_ge(f1_hi, c + 1)
                pool.tensor_tensor(a_lo[:, c % KD, :], slot(c % 2), a_hi[:, c % KD, :].bitcast(F32),
                                   ALU.subtract).then_inc(f1_cut, 1)

        @block.scalar
        def _(act):
            A = nc.scalar.activation

            def norm_square(m, src, junk):
                A(junk, src, ACT.Square, accum_out=row_ss[:, m:m + 1]).then_inc(row_sq, 1)

            def norm_hi(u, dst):
                m, hf = divmod(u % 8, 2)
                act.wait_ge(nt_gained, u + 1)
                A(dst[:, 4 * hf:4 * hf + 4, m * P:(m + 1) * P],
                  slot(TMP + u % 2).rearrange("p (a b) -> p a b", a=4), ACT.Copy).then_inc(nt_hi, 1)

            for m in range(TB):
                act.wait_ge(x_in[m], 16)
                if m >= 1:
                    act.wait_ge(row_sq, m)
                norm_square(m, x_tok[:, m, :], slot(SQ, 2))
            act_cut(0)
            act.wait_ge(gain_t, 1)
            A(gain[:, :], bank(7, 0, 20), ACT.Copy).then_inc(gain_ready, 1)
            act.wait_ge(kw_in, 16)
            A(kw_hi[:, :, :], kw_raw[:, :, :], ACT.Copy).then_inc(kw_hi_done, 1)
            act.wait_ge(gain_ready, 1)
            for j in (16, 18):
                A(gain[:, j:j + 1], gain[:, j:j + 1], ACT.Copy, scale=HD ** -0.5).then_inc(gain_ready, 1)
            for u in range(8):
                norm_hi(u, a_hi)
            act_cut(1)

            def square(n):
                g, m = divmod(n, TB)
                act.wait_ge(proj_done, n + 1)
                if n >= 1:
                    act.wait_ge(ss_done, n)
                w = P if g == KVI else S
                A(slot(2)[:, 0:w], bank(m, 0, w), ACT.Square).then_inc(sq_done, 1)

            def turned(n):
                g, m = divmod(n, TB)
                act.wait_ge(tr_done, n + 1)
                b, t = 4 + n % 2, slice(m * P, (m + 1) * P)
                if g == KVI:
                    A(kT_sa[:, t], bank(b, 0, P), ACT.Copy, scale=gain[:, 19:20])
                    A(qixT[0][:, t], bank(b, P, 2 * P), ACT.Copy)
                    A(qixT[1][:, t], bank(b, 2 * P, 3 * P), ACT.Copy).then_inc(tr_out, 1)
                else:
                    dst, gj = {QSB: (qT_sb, 16), KSB: (kT_sb, 17), QSA: (qT_sa, 18)}[g]
                    A(dst[:, :, t], bank(b).rearrange("p (a b) -> p a b", a=4), ACT.Copy,
                      scale=gain[:, gj:gj + 1]).then_inc(tr_out, 1)

            act.wait_ge(gain_ready, 3)
            act.wait_ge(wT_done, 1)
            A(w_tok[:, :, :], bank(7, 0, TB * IXH).rearrange("p (a b) -> p a b", a=TB), ACT.Copy,
              scale=IXH ** -0.5).then_inc(w_ready, 1)
            for g in range(5):
                if g >= 1:
                    for m in range(TB):
                        turned(4 * (g - 1) + m)
                act_cut(2 * g + 2)
                if g == QSB:
                    for u in range(24):
                        w = (u // 8 + 2) * P
                        act.wait_ge(rel_done, u + 1)
                        if u >= 2:
                            act.wait_ge(score_done, u - 1)
                        A(rel[u % 2][:, 0:w], bank(6 + u % 2, 0, w), ACT.Relu, scale=IXD ** -0.5).then_inc(relu_done, 1)
                if g < 4:
                    for m in range(TB):
                        square(4 * g + m)
                act_cut(2 * g + 3)

            def zset(h):
                return ps[:, 3 * (h % 2) * S:3 * (h % 2) * S + ZW]

            def log_part(h):
                act.wait_ge(z_done, h + 1)
                if h >= 2:
                    act.wait_ge(av_done, h - 1)
                buf = lg[:, h % 2, :]
                A(buf, zset(h), ACT.Abs).then_inc(act_self, 1)
                act.wait_ge(act_self, 2 * h + 1)
                A(buf, buf, ACT.Exp, scale=-1.0).then_inc(act_self, 1)
                act.wait_ge(act_self, 2 * h + 2)
                A(buf, buf, ACT.Ln, bias=1.0).then_inc(ln_done, 1)

            def gate_out(f):
                act.wait_ge(gate_done, f + 1)
                A(gates[:, f, :], bank(7), ACT.Exp, scale=-1.0).then_inc(gate_exp, 1)

            log_part(0)
            for h in range(SBH):
                if h % 2 == 0 and h:
                    act_cut(SL_GATE + 1 + h // 2)
                if h < 7:
                    log_part(h + 1)
                gate_out(h)
                act.wait_ge(tri_done, h + 1)
                A(lg[:, h % 2, :], zset(h), ACT.Exp).then_inc(a_done, 1)
            for n in range(32 + 1):
                if n < 32:
                    w = (n // 8 + 1) * P
                    if n % 8 == 4:
                        act_cut(SL_GATE + 5 + n // 8)
                    act.wait_ge(snmax_done, n + 1)
                    A(sa_s[n % 2][:, 0:w], sa_s[n % 2][:, 0:w], ACT.Exp, bias=snmax[:, n % 2:n % 2 + 1],
                      accum_out=psum_l[:, n % 2:n % 2 + 1]).then_inc(p_done, 1)
                if n >= 1:
                    q = n - 1
                    b, u = q // 8, q // 4
                    act.wait_ge(pt_done, q + 1)
                    if u >= 2:
                        act.wait_ge(pv_done, u - 1)
                    A(pT[u % 2][:, 0:b + 1, (q % 4) * P:(q % 4 + 1) * P],
                      bank(2 + q % 2, 0, (b + 1) * P).rearrange("p (a b) -> p a b", b=P), ACT.Copy).then_inc(pt_out, 1)
                    if q % 4 == 3:
                        gate_out(8 + q // 4)
            act.wait_ge(pv_done, 8)
            act.wait_ge(pt_out, 32)
            act.wait_ge(osb_out, 4)
            for c in range(8):
                if c == 4:
                    act.wait_ge(osa_out, 8)
                A(b_hi[:, c, :], (qT_sb if c < 4 else qT_sa)[:, c % 4, :], ACT.Copy).then_inc(o_hi, 1)
            act_cut(SL_BR + 1)
            for q in range(4):
                if q < 4:
                    act_cut(SL_BR + 2 + q)
                if q % 2:
                    for j in range(4):
                        f = 4 * (q // 2) + j
                        act.wait_ge(mg_sum, f + 1)
                        A(a_hi[:, f, :], gates[:, f, :], ACT.Copy).then_inc(mg_hi, 1)
            act_cut(SL_OUT + 2)
            act_cut(SL_OUT + 3)
            act_cut(SL_FF)
            act_cut(SL_FF + 1)
            for m in range(TB):
                act.wait_ge(wo_out, 4 + m + 1)
                norm_square(TB + m, xres[:, m, :], slot(12, 2) if m % 2 else slot(14, 2))
                if m >= 1:
                    norm_hi(8 + 2 * (m - 1), b_hi)
                    norm_hi(9 + 2 * (m - 1), b_hi)
            norm_hi(14, b_hi)
            norm_hi(15, b_hi)

            def ff1_hidden(c):
                act.wait_ge(f1_done, c + 1)
                A(slot(4 + c % 2), bank(6 + c % 2), ACT.Relu).then_inc(f1_relu, 1)
                act.wait_ge(f1_sq, c + 1)
                A(a_hi[:, c % KD, :], slot(c % 2), ACT.Copy).then_inc(f1_hi, 1)

            for g in range(FG):
                for j in range(8):
                    i = SL_FF + 8 * g + j
                    if j < 4:
                        ff1_hidden(8 * g + 2 * j)
                        ff1_hidden(8 * g + 2 * j + 1)
                    if i + 2 < SL_END:
                        act_cut(i + 2)

        @block.vector
        def _(dve):
            count = [0]

            def link(ins):
                count[0] += 1
                ins.then_inc(dve_self, 1)
                dve.wait_ge(dve_self, count[0])

            V = nc.vector

            dve.wait_ge(ident_done, 1)
            dve.wait_ge(const_made, 1)
            V.tensor_copy(ident_r, ident[:, :])
            V.tensor_copy(const_r[:, 1:4, :], const_f[:, :, :]).then_inc(const_cut, 1)

            def norm_scale(m, dst, src):
                dve.wait_ge(row_ready, m + 1)
                V.tensor_scalar(dst, src, row_r[:, m:m + 1], None, ALU.mult).then_inc(row_scaled, 1)

            def norm_gain(u, g0):
                hf = u % 2
                dve.wait_ge(nt_done, u + 1)
                if u >= 2:
                    dve.wait_ge(nt_cut, u - 1)
                V.tensor_tensor(slot(TMP + u % 2).rearrange("p (a b) -> p a b", a=4),
                                bank(4 + u % 2).rearrange("p (a b) -> p a b", a=4),
                                gain[:, g0 + 4 * hf:g0 + 4 * hf + 4].unsqueeze(2).to_broadcast([P, 4, P]),
                                ALU.mult).then_inc(nt_gained, 1)

            def norm_lo(u, hi, lo):
                m, hf = divmod(u % 8, 2)
                at = (slice(None), slice(4 * hf, 4 * hf + 4), slice(m * P, (m + 1) * P))
                dve.wait_ge(nt_hi, u + 1)
                V.tensor_tensor(lo[at], slot(TMP + u % 2).rearrange("p (a b) -> p a b", a=4), hi[at].bitcast(F32),
                                ALU.subtract).then_inc(nt_cut, 1)

            for m in range(TB):
                norm_scale(m, x_tok[:, m, :], x_tok[:, m, :])
            dve.wait_ge(gain_ready, 1)
            for u in range(9):
                if u < 8:
                    norm_gain(u, 0)
                if u >= 1:
                    norm_lo(u - 1, a_hi, a_lo)
                if u == 1:
                    dve_cut(0)
            dve.wait_ge(kw_hi_done, 1)
            V.tensor_tensor(kw_lo[:, :, :], kw_raw[:, :, :], kw_hi[:, :, :].bitcast(F32), ALU.subtract).then_inc(kw_cut, 1)
            dve_cut(1)

            def topk_steps():
                for b in range(1, TB):
                    dve.wait_ge(causal_done, b)
                    for r in range(TOPK // 8):
                        link(V.max(best8[:, :], topmask[b]))
                        link(V.match_replace(out=topmask[b], in_to_replace=best8[:, :], in_values=topmask[b],
                                             imm_value=TAKEN))
                        yield
                    V.tensor_scalar(topmask[b], topmask[b], TAKEN * 0.5, MASKED, ALU.is_gt, ALU.mult).then_inc(mask_ready, 1)
                    yield

            steps = topk_steps()

            def topk(n):
                for _ in range(n):
                    next(steps, None)

            def head_sums(n):
                g, m = divmod(n, TB)
                nh = 2 if g == KVI else 8
                dve.wait_ge(sq_done, n + 1)
                if n >= 2:
                    dve.wait_ge(hr_done, n - 1)
                V.tensor_reduce(head_ss[:, n % 2, 0:nh], slot(2)[:, 0:nh * HD].rearrange("p (h d) -> p h d", d=HD),
                                AX.X, ALU.add).then_inc(ss_done, 1)

            def head_scaled(n):
                g, m = divmod(n, TB)
                nh = 2 if g == KVI else 8
                if n >= 2:
                    dve.wait_ge(tr_done, n - 1)
                dve.wait_ge(hr_done, n + 1)
                r = head_r[:, n % 2, 0:nh]
                if g == KVI:
                    V.tensor_copy(v_sa[:, m, :], bank(m, P, 2 * P))
                    V.tensor_copy(tok[n % 2][:, P:3 * P], bank(m, 2 * P, 4 * P))
                if g == QSA:
                    V.tensor_tensor(tok[n % 2].rearrange("p (r g d) -> p g r d", g=2, d=HD),
                                    bank(m).rearrange("p (g r d) -> p g r d", g=2, d=HD),
                                    r.rearrange("p (g r) -> p g r", g=2).unsqueeze(3).to_broadcast([P, 2, 4, HD]),
                                    ALU.mult).then_inc(proj_out, 1)
                else:
                    V.tensor_tensor(tok[n % 2][:, 0:nh * HD].rearrange("p (h d) -> p h d", d=HD),
                                    bank(m, 0, nh * HD).rearrange("p (h d) -> p h d", d=HD),
                                    r.unsqueeze(2).to_broadcast([P, nh, HD]), ALU.mult).then_inc(proj_out, 1)

            dve.wait_ge(kix_done, 1)
            V.tensor_copy(kw_sb[0:40, :], bank(6)[0:40, :]).then_inc(kix_out, 1)
            for g in range(5):
                dve_cut(2 * g + 2)
                if g == QSB:
                    dve.wait_ge(w_ready, 1)
                    for u in range(24):
                        b, h = u // 8 + 1, u % 8
                        dve.wait_ge(relu_done, u + 1)
                        src, wgt = rel[u % 2][:, 0:(b + 1) * P], w_tok[:, b, h:h + 1]
                        if h == 0:
                            V.tensor_scalar(topmask[b], src, wgt, None, ALU.mult).then_inc(score_done, 1)
                        else:
                            dve.wait_ge(score_done, u)
                            V.scalar_tensor_tensor(out=topmask[b], in0=src, scalar=wgt, in1=topmask[b],
                                                   op0=ALU.mult, op1=ALU.add).then_inc(score_done, 1)
                if g < 4:
                    for m in range(TB):
                        head_sums(4 * g + m)
                        head_scaled(4 * g + m)
                else:
                    for m in range(TB):
                        dve.wait_ge(proj_done, 16 + m + 1)
                        V.tensor_copy(v_sb[:, m, :], bank(m)).then_inc(proj_out, 1)
                dve_cut(2 * g + 3)
                if g >= KSB:
                    topk(6)

            def zset(h):
                return ps[:, 3 * (h % 2) * S:3 * (h % 2) * S + ZW]

            def softplus(h):
                buf = lg[:, h % 2, :]
                dve.wait_ge(ln_done, h + 1)
                link(V.scalar_tensor_tensor(out=buf, in0=zset(h), scalar=0.0, in1=buf, op0=ALU.max, op1=ALU.add))
                if h >= 1:
                    dve.wait_ge(tri_done, h)
                link(V.tensor_copy(sp_hi[:, :], buf))
                V.tensor_tensor(sp_lo[:, :], buf, sp_hi[:, :].bitcast(F32), ALU.subtract).then_inc(sp_done, 1)

            def gate_recip(f):
                dve.wait_ge(gate_p1, f + 1)
                V.reciprocal(gates[:, f, :], gates[:, f, :]).then_inc(gate_ready, 1)

            for h in range(SBH):
                softplus(h)
                if h % 2 == 0 and h:
                    dve_cut(SL_GATE + 1 + h // 2)
                topk(5)
                if h % 2:
                    dve.wait_ge(av_done, h + 1)
                    V.tensor_copy(qT_sb[:, h // 2, :], bank(6)).then_inc(osb_out, 1)
                if h >= 1:
                    gate_recip(h - 1)
            topk(60)
            gate_recip(7)
            for n in range(32 + 1):
                if n < 32:
                    w = (n // 8 + 1) * P
                    if n % 8 == 4:
                        dve_cut(SL_GATE + 5 + n // 8)
                    dve.wait_ge(s_done, n + 1)
                    dve.wait_ge(bias_done, n + 1)
                    if n >= 2:
                        dve.wait_ge(pt_done, n - 1)
                    V.tensor_tensor_reduce(out=sa_s[n % 2][:, 0:w], in0=bank(n % 2, 0, w), in1=sa_bias[n % 2][:, 0:w],
                                           scale=1.0, scalar=-3.0e38, op0=ALU.add, op1=ALU.max,
                                           accum_out=smax[:, n % 2:n % 2 + 1]).then_inc(smax_done, 1)
                    dve.wait_ge(smax_done, n + 1)
                    V.tensor_scalar(snmax[:, n % 2:n % 2 + 1], smax[:, n % 2:n % 2 + 1], -1.0, None,
                                    ALU.mult).then_inc(snmax_done, 1)
                if n >= 1:
                    q = n - 1
                    w = (q // 8 + 1) * P
                    dve.wait_ge(p_done, q + 1)
                    link(V.reciprocal(rcp_l[:, q % 2:q % 2 + 1], psum_l[:, q % 2:q % 2 + 1]))
                    V.tensor_scalar(sa_s[q % 2][:, 0:w], sa_s[q % 2][:, 0:w], rcp_l[:, q % 2:q % 2 + 1], None,
                                    ALU.mult).then_inc(pn_done, 1)
                if n >= 6 and n % 4 == 2 or n == 32:
                    for u in ([n // 4 - 1 - (n == 32)] if n < 32 else [7]):
                        b, g = divmod(u, 2)
                        dve.wait_ge(pv_done, u + 1)
                        V.tensor_copy(qT_sa[64 * g:64 * g + 64, :, b * P:(b + 1) * P],
                                      bank(4 + u % 2)[64 * g:64 * g + 64, :].rearrange("p (a b) -> p a b", a=4)
                                      ).then_inc(osa_out, 1)
                        gate_recip(8 + u)
            for c in range(8):
                dve.wait_ge(o_hi, c + 1)
                V.tensor_tensor(b_lo[:, c, :], (qT_sb if c < 4 else qT_sa)[:, c % 4, :],
                                b_hi[:, c, :].bitcast(F32), ALU.subtract).then_inc(o_cut, 1)
            dve_cut(SL_BR + 1)
            for q in range(4):
                dve_cut(SL_BR + 2 + q)
                for j in range(4):
                    f = 8 * (q % 2) + 4 * (q // 2) + j
                    dve.wait_ge(br_done, 4 * q + j + 1)
                    V.tensor_tensor(gates[:, f, :], bank(4 * (q % 2) + j), gates[:, f, :], ALU.mult).then_inc(br_out, 1)
                if q % 2:
                    for j in range(4):
                        f = 4 * (q // 2) + j
                        dve.wait_ge(mg_hi, f + 1)
                        V.tensor_tensor(a_lo[:, f, :], gates[:, f, :], a_hi[:, f, :].bitcast(F32),
                                        ALU.subtract).then_inc(mg_cut, 1)
            dve.wait_ge(x2_in, 16)
            dve_cut(SL_OUT + 2)
            for n in range(2):
                for m in range(TB):
                    dve.wait_ge(wo_done, 4 * n + m + 1)
                    part = xres[:, m, n * 512:(n + 1) * 512]
                    V.tensor_tensor(part, bank(m), part, ALU.add).then_inc(wo_out, 1)
                    if n == 1:
                        norm_scale(TB + m, slot(2 * m, 2), xres[:, m, :])
                        if m >= 1:
                            for u in (8 + 2 * m - 2, 8 + 2 * m - 1):
                                norm_gain(u, 8)
                                norm_lo(u, b_hi, b_lo)
                if n == 0:
                    dve_cut(SL_OUT + 3)
                    dve_cut(SL_FF)
            for u in (14, 15):
                norm_gain(u, 8)
                norm_lo(u, b_hi, b_lo)
            dve_cut(SL_FF + 1)

            def ff1_square(c):
                dve.wait_ge(f1_relu, c + 1)
                if c >= 2:
                    dve.wait_ge(f1_cut, c - 1)
                V.scalar_tensor_tensor(out=slot(c % 2), in0=bank(6 + c % 2), scalar=0.0, in1=slot(4 + c % 2),
                                       op0=ALU.max, op1=ALU.mult).then_inc(f1_sq, 1)

            for g in range(FG):
                for j in range(8):
                    i = SL_FF + 8 * g + j
                    if j < 4:
                        ff1_square(8 * g + 2 * j)
                        ff1_square(8 * g + 2 * j + 1)
                    if i + 2 < SL_END:
                        dve_cut(i + 2)
                    if j in (5, 7):
                        n = (j - 5) // 2
                        for m in range(TB):
                            dve.wait_ge(f2_done, 8 * g + 4 * n + m + 1)
                            part = xres[:, m, n * 512:(n + 1) * 512]
                            V.tensor_tensor(part, bank(m), part, ALU.add).then_inc(f2_out, 1)

        @block.tensor
        def _(pe):
            T = nc.tensor

            def norm_turn(m, src):
                pe.wait_ge(row_scaled, m + 1)
                for hf in range(2):
                    u = 2 * m + hf
                    if u >= 2:
                        pe.wait_ge(nt_gained, u - 1)
                    for k in range(4):
                        t = T.transpose(bank(4 + u % 2, k * P, (k + 1) * P),
                                        src[:, (4 * hf + k) * P:(4 * hf + k + 1) * P], ident[:, :])
                    t.then_inc(nt_done, 1)

            pe.wait_ge(ident_done, 1)
            pe.wait_ge(gains_in, 160)
            T.transpose(bank(7, 0, 20), gain_rows[:, :], ident[0:20, 0:20]).then_inc(gain_t, 1)
            for m in range(TB):
                norm_turn(m, x_tok[:, m, :])

            def slab_ready(i):
                pe.wait_ge(lo_done, i + 1)

            def project(g, half):
                i = SL_PROJ + 2 * g + half
                slab_ready(i)
                for m in range(TB):
                    if half == 0 and g >= 1:
                        pe.wait_ge(proj_out, 4 * (g - 1) + m + 1)
                    for k in range(4):
                        kk, t = 4 * half + k, slice(m * P, (m + 1) * P)
                        mm = moving_weights(i, k, bank(m), a_hi[:, kk, t], a_lo[:, kk, t],
                                            start=(kk == 0), stop=(kk == 7))
                    if half == 1:
                        mm.then_inc(proj_done, 1)
                    elif g >= 1:
                        turn(4 * (g - 1) + m)
                if half == 0:
                    mm.then_inc(half_done, 1)

            def turn(n):
                g, m = divmod(n, TB)
                pe.wait_ge(proj_out, n + 1)
                if n >= 2:
                    pe.wait_ge(tr_out, n - 1)
                for k in range(3 if g == KVI else 4):
                    t = T.transpose(bank(4 + n % 2, k * P, (k + 1) * P), tok[n % 2][:, k * P:(k + 1) * P], ident[:, :])
                t.then_inc(tr_done, 1)

            pe.wait_ge(nt_cut, 8)
            pe.wait_ge(kw_cut, 1)
            for k in range(KD):
                T.matmul(bank(6)[0:40, :], kw_hi[:, k, :], a_hi[:, k, :], start=(k == 0), stop=False)
                T.matmul(bank(6)[0:40, :], kw_hi[:, k, :], a_lo[:, k, :], start=False, stop=False)
                mm = T.matmul(bank(6)[0:40, :], kw_lo[:, k, :], a_hi[:, k, :], start=False, stop=(k == KD - 1))
            mm.then_inc(kix_done, 1)
            pe.wait_ge(kix_out, 1)
            for m in range(TB):
                t = T.transpose(bank(7, m * IXH, (m + 1) * IXH), kw_sb[32:40, m * P:(m + 1) * P], ident[32:40, 32:40])
            t.then_inc(wT_done, 1)

            def indexer():
                pe.wait_ge(tr_out, 4)
                pe.wait_ge(kix_rep, 64)
                pe.wait_ge(w_ready, 1)
                for u in range(24):
                    b, h = u // 8 + 1, u % 8
                    if u >= 2:
                        pe.wait_ge(relu_done, u - 1)
                    q = 32 * (h % 4)
                    T.matmul(bank(6 + u % 2, 0, (b + 1) * P), qixT[h // 4][q:q + 32, b * P:(b + 1) * P],
                             kixT[q:q + 32, 0:(b + 1) * P], start=True, stop=True).then_inc(rel_done, 1)

            for g in range(5):
                project(g, 0)
                if g == QSB:
                    indexer()
                project(g, 1)

            def zt(h, i, t0=None):
                t0 = i if t0 is None else t0
                a = 3 * (h % 2) * S + ZCOL[i]
                return ps[:, a + (t0 - i) * P:a + (4 - i) * P]

            def logits(h):
                c, p0 = h // 2, 64 * (h % 2)
                if h >= 2:
                    pe.wait_ge(a_done, h - 1)
                for i in range(4):
                    T.matmul(zt(h, i), kT_sb[p0:p0 + 64, c, i * P:(i + 1) * P], qT_sb[p0:p0 + 64, c, i * P:S],
                             start=(i != 3), stop=False, skip_group_check=True)
                    mm = T.matmul(zt(h, i)[:, 0:P], ident_r, mask_r, start=False, stop=False, skip_group_check=True)
                mm.then_inc(z_done, 1)

            def sum_later(h):
                pe.wait_ge(sp_done, h + 1)
                for i in range(4):
                    for j in range(i, 4):
                        a = ZCOL[j]
                        for n, part in enumerate((sp_hi, sp_lo)):
                            mm = T.matmul(zt(h, i, j), tri_r if i == j else ones_r, part[:, a:a + (4 - j) * P],
                                          start=False, stop=(j == 3 and n == 1), skip_group_check=True)
                mm.then_inc(tri_done, 1)

            def weighted_values(h):
                p0 = 64 * (h % 2)
                pe.wait_ge(a_done, h + 1)
                if h >= 2 and h % 2 == 0:
                    pe.wait_ge(osb_out, h // 2)
                for i in range(4):
                    mm = T.matmul(bank(6, i * P, S)[p0:p0 + 64, :], v_sb[:, i, h * HD:(h + 1) * HD],
                                  lg[:, h % 2, ZCOL[i]:ZCOL[i] + (4 - i) * P], start=(i == 0), stop=(i == 3),
                                  skip_group_check=True)
                mm.then_inc(av_done, 1)

            def gate(f):
                i = SL_GATE + f // 2
                slab_ready(i)
                if f >= 1:
                    pe.wait_ge(gate_exp, f)
                for k in range(KD):
                    mm = stationary_weights(i, k, KD, (f % 2) * P, bank(7), a_hi[:, k, :], a_lo[:, k, :],
                                            start=(k == 0), stop=(k == KD - 1))
                mm.then_inc(gate_done, 1)

            pe.wait_ge(const_cut, 1)
            pe.wait_ge(tr_out, 16)
            pe.wait_ge(proj_out, 20)
            pe.wait_ge(score_done, 24)
            logits(0)
            for h in range(SBH):
                if h < 7:
                    logits(h + 1)
                gate(h)
                sum_later(h)
                weighted_values(h)

            def sa_scores(n):
                b, h = divmod(n, 8)
                g, r = divmod(h, 4)
                if n >= 2:
                    pe.wait_ge(smax_done, n - 1)
                T.matmul(bank(n % 2, 0, (b + 1) * P), qT_sa[64 * g:64 * g + 64, r, b * P:(b + 1) * P],
                         kT_sa[64 * g:64 * g + 64, 0:(b + 1) * P], start=True, stop=True).then_inc(s_done, 1)

            def sa_turn(n):
                b = n // 8
                pe.wait_ge(pn_done, n + 1)
                if n >= 2:
                    pe.wait_ge(pt_out, n - 1)
                for i in range(b + 1):
                    t = T.transpose(bank(2 + n % 2, i * P, (i + 1) * P), sa_s[n % 2][:, i * P:(i + 1) * P], ident[:, :])
                t.then_inc(pt_done, 1)

            def sa_values(u):
                b, g = divmod(u, 2)
                pe.wait_ge(pt_out, 4 * u + 4)
                if u >= 2:
                    pe.wait_ge(osa_out, u - 1)
                for i in range(b + 1):
                    mm = T.matmul(bank(4 + u % 2)[64 * g:64 * g + 64, :], v_sa[:, i, 64 * g:64 * g + 64],
                                  pT[u % 2][:, i, :], start=(i == 0), stop=(i == b))
                mm.then_inc(pv_done, 1)

            pe.wait_ge(a_done, 8)
            sa_scores(0)
            sa_scores(1)
            for n in range(32):
                sa_turn(n)
                if n < 30:
                    sa_scores(n + 2)
                if n % 4 == 3:
                    gate(8 + n // 4)
                    sa_values(n // 4)

            pe.wait_ge(gate_exp, 16)
            pe.wait_ge(osa_out, 8)
            for q in range(4):
                i = SL_BR + q
                slab_ready(i)
                for j in range(4):
                    if q >= 2:
                        pe.wait_ge(br_out, 4 * (q - 2) + j + 1)
                    for k in range(4):
                        c = 4 * (q % 2) + k
                        if q < 2 and j == 0:
                            pe.wait_ge(o_cut, c + 1)
                        mm = stationary_weights(i, k, 4, j * P, bank(4 * (q % 2) + j), b_hi[:, c, :], b_lo[:, c, :],
                                                start=(k == 0), stop=(k == 3))
                    mm.then_inc(br_done, 1)

            for q in range(4):
                n, half = divmod(q, 2)
                i = SL_OUT + q
                slab_ready(i)
                for m in range(TB):
                    if half == 0:
                        pe.wait_ge(br_out, 12) if n == 0 else pe.wait_ge(wo_out, m + 1)
                    for k in range(4):
                        kk, t = 4 * half + k, slice(m * P, (m + 1) * P)
                        if n == 0 and m == 0:
                            pe.wait_ge(mg_cut, kk + 1)
                        mm = moving_weights(i, k, bank(m), a_hi[:, kk, t], a_lo[:, kk, t],
                                            start=(kk == 0), stop=(kk == 7))
                    if half == 1:
                        mm.then_inc(wo_done, 1)
                if half == 0:
                    mm.then_inc(half_done, 1)
            for m in range(TB):
                norm_turn(TB + m, slot(2 * m, 2))

            pe.wait_ge(nt_cut, 16)
            for g in range(FG):
                for j in range(4):
                    i = SL_FF + 8 * g + j
                    slab_ready(i)
                    for o in range(2):
                        c = 8 * g + 2 * j + o
                        if c >= 2:
                            pe.wait_ge(f1_sq, c - 1)
                        for k in range(KD):
                            mm = stationary_weights(i, k, KD, o * P, bank(6 + c % 2), b_hi[:, k, :], b_lo[:, k, :],
                                                    start=(k == 0), stop=(k == KD - 1))
                        mm.then_inc(f1_done, 1)
                for q in range(4):
                    n, half = divmod(q, 2)
                    i = SL_FF + 8 * g + 4 + q
                    slab_ready(i)
                    for m in range(TB):
                        e = 8 * g + 4 * n + m
                        if half == 0:
                            if e >= 4:
                                pe.wait_ge(f2_out, e - 3)
                            else:
                                pe.wait_ge(wo_out, 5 + m)
                        for k in range(4):
                            kk, t = 4 * half + k, slice(m * P, (m + 1) * P)
                            if n == 0 and m == 0:
                                pe.wait_ge(f1_cut, 8 * g + kk + 1)
                            mm = moving_weights(i, k, bank(m), a_hi[:, kk, t], a_lo[:, kk, t],
                                                start=(kk == 0), stop=(kk == 7))
                        if half == 1:
                            mm.then_inc(f2_done, 1)
                    if half == 0:
                        mm.then_inc(half_done, 1)


_INS = ["x", "norm_mix", "w_in", "q_norm_sb", "k_norm_sb", "q_norm_sa", "k_norm_sa",
        "w_branch_sb", "w_branch_sa", "w_out", "norm_mlp", "w_ff1", "w_ff2"]
_OUTS = [((1, S, D), "float32")]


def kernel(**inputs):
    import numpy as _np
    import concourse.bacc as _bacc
    from concourse import mybir as _mybir
    from concourse.bass_utils import run_bass_kernel_spmd as _run

    nc = _bacc.Bacc("TRN2", target_bir_lowering=False, num_devices=1)
    arrays, args = {}, []
    for name in _INS:
        a = _np.ascontiguousarray(inputs[name])
        arrays[f"in_{name}_dram"] = a
        args.append(nc.dram_tensor(f"in_{name}_dram", a.shape, _mybir.dt.from_np(a.dtype), kind="ExternalInput").ap())
    for i, (shape, dtype) in enumerate(_OUTS):
        dt = _mybir.dt.from_np(_np.dtype(dtype))
        args.append(nc.dram_tensor(f"out_{i}_dram", shape, dt, kind="ExternalOutput").ap())
    block_kernel(nc, *args)
    r = _run(nc, [arrays], core_ids=[0])
    got = tuple(r.results[0][f"out_{i}_dram"] for i in range(len(_OUTS)))
    return got[0]
```

```python
from contextlib import ExitStack

import concourse.bass as bass
from concourse import mybir

ALU = mybir.AluOpType
ACT = mybir.ActivationFunctionType
AX = mybir.AxisListType
F32 = mybir.dt.float32
F32R = mybir.dt.float32r
I32 = mybir.dt.int32
BF16 = mybir.dt.bfloat16

P = 128
S = 512
D = 1024
FF = 4 * D
TB = S // P
KD = D // P
HD = 64
SBH = 8
SAH, SAKV = 8, 2
GQ = SAH // SAKV
IXH, IXD = 8, 32
TOPK = min(256, S // 4)
EPS = 1e-6
MASKED = -1e30
TAKEN = -3e38

C_QSB, C_KSB, C_VSB, C_QSA, C_KVI = 0, 512, 1024, 1536, 2048
C_KW = 2560
C_GATE = 2600

RAW, CUT, SLAB = 4, 2, 2048

GROUPS = [C_KVI, C_QSB, C_KSB, C_QSA, C_VSB]
KVI, QSB, KSB, QSA, VSB = range(5)
SL_PROJ = 0
SL_GATE = SL_PROJ + 2 * len(GROUPS)
SL_BR = SL_GATE + 8
SL_OUT = SL_BR + 4
SL_FF = SL_OUT + 4
FG = 4
SL_END = SL_FF + 8 * FG

ZCOL = [0, 512, 1024, 896]
ZW = 1280


def block_kernel(nc, x, norm_mix, w_in, q_norm_sb, k_norm_sb, q_norm_sa, k_norm_sa,
                 w_branch_sb, w_branch_sa, w_out, norm_mlp, w_ff1, w_ff2, out):
    ctx = ExitStack()
    with ctx:
        def sb(name, shape, dt, where=ctx):
            return where.enter_context(nc.sbuf_tensor(name, shape, dt))

        def sem(name):
            return ctx.enter_context(nc.semaphore(name))

        raw = sb("raw", [P, RAW, SLAB], F32)
        cut_hi = sb("cut_hi", [P, CUT, SLAB], F32R)
        cut_lo = sb("cut_lo", [P, CUT, SLAB], F32R)
        a_hi = sb("a_hi", [P, KD, S], F32R)
        a_lo = sb("a_lo", [P, KD, S], F32R)
        gates = sb("gates", [P, 16, S], F32)
        qz_sb = sb("qz_sb", [P, SBH, S], F32)
        oT_sb = qz_sb[:, 0::2, :]
        qT_sa = sb("qT_sa", [P, 4, S], F32)
        ident = sb("ident", [P, P], F32)
        const_f = sb("const_f", [P, 3, P], F32)
        tri_f, ones_f, mask_f = (const_f[:, j, :] for j in range(3))
        const_r = sb("const_r", [P, 2, P], F32R)
        tri_r, ones_r = const_r[:, 0, :], const_r[:, 1, :]
        const_b = sb("const_b", [P, 2, P], BF16)
        ident_b, mask_b = const_b[:, 0, :], const_b[:, 1, :]
        dist = sb("dist", [P, S], F32)
        dist_i = dist[:, :].bitcast(I32)
        gain = sb("gain", [P, 20], F32)
        w_tok = sb("w_tok", [P, TB, IXH], F32)
        row_ss = sb("row_ss", [P, 2 * TB], F32)
        row_ms = sb("row_ms", [P, 2 * TB], F32)
        row_r = sb("row_r", [P, 2 * TB], F32)
        head_ss = sb("head_ss", [P, 2, 8], F32)
        head_ms = sb("head_ms", [P, 2, 8], F32)
        head_r = sb("head_r", [P, 2, 8], F32)
        minus_half = sb("minus_half", [P, 8], F32)
        best8 = sb("best8", [P, 8], F32)
        snmax = sb("snmax", [P, 4], F32)
        sum_p = sb("sum_p", [P, 4], F32)
        rcp_l = sb("rcp_l", [P, 4], F32)

        early = ExitStack()
        kv_sb = sb("kv_sb", [P, 2, 4, S], F32, early)
        kT_sb, v_sb = kv_sb[:, 0], kv_sb[:, 1]
        kz_sa = sb("kz_sa", [P, SAKV, S], F32, early)
        v_sa = sb("v_sa", [P, TB, P], F32, early)
        lg = sb("lg", [P, 2, ZW], F32, early)
        sp_hi = sb("sp_hi", [P, ZW], F32R, early)
        sp_lo = sb("sp_lo", [P, ZW], F32R, early)
        topm = sb("topm", [P, ZW], F32, early)
        early.close()
        late = ExitStack()
        b_hi = sb("b_hi", [P, KD, S], F32R, late)
        b_lo = sb("b_lo", [P, KD, S], F32R, late)
        cut3_hi = sb("cut3_hi", [P, SLAB], F32R, late)
        cut3_lo = sb("cut3_lo", [P, SLAB], F32R, late)
        late.close()

        def slot(j, n=1):
            return gates[:, j:j + n, :].rearrange("p a b -> p (a b)")
        x_tok = gates[:, 0:8, :].rearrange("p (m a) b -> p m (a b)", m=TB)
        xres = x_tok
        SQ = 8

        def rows_t(u):
            return slot((10 if u < 8 else 12) + u % 2)
        xn2 = [slot(8, 2), slot(10, 2)]
        ff_sq, ff_relu = [slot(12), slot(13)], [slot(14), slot(15)]
        tok = [slot(0), slot(1)]
        qixT = [slot(3), slot(4)]
        kw_sb = slot(6)
        kz_ix = gates[:, 12:16, :]
        kw_raw = lg[:, 0, 0:320].rearrange("p (k c) -> p k c", k=KD)
        gain_rows = lg[0:20, 0, 384:512]
        kw_hi, kw_lo = (t[:, 0:320].rearrange("p (k c) -> p k c", k=KD) for t in (sp_hi, sp_lo))
        rel = [slot(7), slot(8)]
        MOFF = [0, 128, 384, 768]
        topmask = [topm[:, MOFF[b]:MOFF[b] + (b + 1) * P] for b in range(TB)]
        weights = [gates[:, a:a + 3, :].rearrange("p a b -> p (a b)")[:, 0:ZW] for a in (8, 11)]
        lg_flat = lg[:, :, :].rearrange("p a b -> p (a b)")
        sa_s = [lg_flat[:, j * S:(j + 1) * S] for j in range(4)]
        sa_bias = [qz_sb[:, 2 * j + 1, :] for j in range(4)]
        pT = [kv_sb[:, j].rearrange("p a b -> p (a b)").rearrange("p (g i r t) -> p g i r t", g=SAKV, i=4, r=2)
              for j in range(2)]

        ps = ctx.enter_context(nc.psum_tensor("ps", [P, 8 * S], F32))

        def bank(j, a=0, b=S):
            return ps[:, j * S + a:j * S + b]

        x_in = [sem(f"x_in{m}") for m in range(TB)]
        x2_in = sem("x2_in")
        gains_in, kw_in = sem("gains_in"), sem("kw_in")
        raw_in = [sem(f"raw_in{j}") for j in range(RAW)]
        hi_done, lo_done, half_done = sem("hi_done"), sem("lo_done"), sem("half_done")
        pool_self, dve_self, act_self = sem("pool_self"), sem("dve_self"), sem("act_self")
        ident_done, const_made, const_cut, dist_done = sem("ident_done"), sem("const_made"), sem("const_cut"), sem("dist_done")
        gain_t, gain_ready = sem("gain_t"), sem("gain_ready")
        kw_hi_done, kw_cut = sem("kw_hi_done"), sem("kw_cut")
        row_sq, row_ready, row_scaled = sem("row_sq"), sem("row_ready"), sem("row_scaled")
        nt_done, nt_gained, nt_hi, nt_cut = sem("nt_done"), sem("nt_gained"), sem("nt_hi"), sem("nt_cut")
        proj_done, sq_done, ss_done, hr_done = sem("proj_done"), sem("sq_done"), sem("ss_done"), sem("hr_done")
        proj_out, tr_done, tr_out = sem("proj_out"), sem("tr_done"), sem("tr_out")
        kix_done, kix_out, kix_rep, wT_done, w_ready = sem("kix_done"), sem("kix_out"), sem("kix_rep"), sem("wT_done"), sem("w_ready")
        rel_done, relu_done, score_done, causal_done, mask_ready, kix_zero, q_zero = sem("rel_done"), sem("relu_done"), sem("score_done"), sem("causal_done"), sem("mask_ready"), sem("kix_zero"), sem("q_zero")
        mask0 = sem("mask0")
        z_done, ln_done, sp_done, tri_done, a_done, av_done, osb_out = (sem(n) for n in (
            "z_done", "ln_done", "sp_done", "tri_done", "a_done", "av_done", "osb_out"))
        gate_done, gate_exp, gate_ln, gsb_ready, gsa_ready = (sem(n) for n in (
            "gate_done", "gate_exp", "gate_ln", "gsb_ready", "gsa_ready"))
        bias_done, s_done, smax_done, p_done, pn_done, pt_done, pt_out, pv_done, osa_out = (
            sem(n) for n in ("bias_done", "s_done", "smax_done", "p_done", "pn_done",
                             "pt_done", "pt_out", "pv_done", "osa_out"))
        o_hi, o_cut = sem("o_hi"), sem("o_cut")
        br_done, br_out, mg_sum, mg_hi, mg_cut = (sem(n) for n in ("br_done", "br_out", "mg_sum", "mg_hi", "mg_cut"))
        wo_done, wo_out = sem("wo_done"), sem("wo_out")
        f1_done, f1_relu, f1_sq, f1_hi, f1_cut = (sem(n) for n in ("f1_done", "f1_relu", "f1_sq", "f1_hi", "f1_cut"))
        f2_done, f2_out, y_out = sem("f2_done"), sem("f2_out"), sem("y_out")

        def rows(w, r0, nk, c0, nc_):
            return w[r0:r0 + nk * P, c0:c0 + nc_].rearrange("(k p) c -> p k c", p=P)

        x_d = x[0]
        win, wsb, wsa, wout, wf1, wf2 = w_in[0], w_branch_sb[0], w_branch_sa[0], w_out[0], w_ff1[0], w_ff2[0]

        def slab_source(i):
            if i < SL_GATE:
                g, half = divmod(i - SL_PROJ, 2)
                return [(0, P, 4, rows(win, half * 512, 4, GROUPS[g], 512))]
            if i < SL_BR:
                return [(0, P, 8, rows(win, 0, 8, C_GATE + 256 * (i - SL_GATE), 256))]
            if i < SL_OUT:
                q = i - SL_BR
                c0 = 512 * (q // 2)
                if q % 2 == 0:
                    return [(0, P, 4, rows(wsb, 0, 4, c0, 512))]
                return [(64 * g, 64, 4, wsa[256 * g:256 * g + 256, c0:c0 + 512].rearrange("(r d) c -> d r c", d=HD))
                        for g in range(SAKV)]
            if i < SL_FF:
                n, half = divmod(i - SL_OUT, 2)
                return [(0, P, 4, rows(wout, half * 512, 4, n * 512, 512))]
            g, j = divmod(i - SL_FF, 8)
            if j < 4:
                return [(0, P, 8, rows(wf1, 0, 8, 1024 * g + 256 * j, 256))]
            n, half = divmod(j - 4, 2)
            return [(0, P, 4, rows(wf2, 1024 * g + half * 512, 4, n * 512, 512))]

        def slab_arrived(i):
            n = sum(len(slab_source(j)) for j in range(i % RAW, i + 1, RAW))
            return raw_in[i % RAW], 16 * n

        def slab_used(i):
            if i < SL_GATE:
                g, half = divmod(i - SL_PROJ, 2)
                return (proj_done, 4 * g + 4) if half or g == 0 else (half_done, g)
            if i < SL_BR:
                return gate_done, 2 * (i - SL_GATE) + 2
            if i < SL_OUT:
                return br_done, 4 * (i - SL_BR) + 4
            if i < SL_FF:
                n, half = divmod(i - SL_OUT, 2)
                return (wo_done, 4 * n + 4) if half or n == 1 else (half_done, len(GROUPS))
            g, j = divmod(i - SL_FF, 8)
            if j < 4:
                return f1_done, 8 * g + 2 * j + 2
            n, half = divmod(j - 4, 2)
            return (f2_done, 8 * g + 4 * n + 4) if half else (half_done, len(GROUPS) + 2 * g + n + 1)

        def cut_slot(i, part, k, nk):
            w = SLAB // nk
            slab = part[:, i % CUT, :]
            if i == SL_FF:
                slab = cut3_hi if part is cut_hi else cut3_lo
            return slab[:, k * w:(k + 1) * w]

        def act_cut(i):
            nc.scalar.wait_ge(*slab_arrived(i))
            if i >= CUT and i != SL_FF:
                nc.scalar.wait_ge(*slab_used(i - CUT))
            nc.scalar.activation(cut_slot(i, cut_hi, 0, 1), raw[:, i % RAW, :], ACT.Copy).then_inc(hi_done, 1)

        def dve_cut(i):
            nc.vector.wait_ge(hi_done, i + 1)
            nc.vector.tensor_tensor(cut_slot(i, cut_lo, 0, 1), raw[:, i % RAW, :], cut_slot(i, cut_hi, 0, 1).bitcast(F32),
                                    ALU.subtract).then_inc(lo_done, 1)

        def stationary_weights(i, k, nk, col, dst, rhs_hi, rhs_lo, start, stop):
            w_hi = cut_slot(i, cut_hi, k, nk)[:, col:col + P]
            w_lo = cut_slot(i, cut_lo, k, nk)[:, col:col + P]
            nc.tensor.matmul(dst, w_hi, rhs_hi, start=start, stop=False)
            nc.tensor.matmul(dst, w_hi, rhs_lo, start=False, stop=False)
            return nc.tensor.matmul(dst, w_lo, rhs_hi, start=False, stop=stop)

        def moving_weights(i, k, dst, l_hi, l_lo, start, stop):
            w_hi, w_lo = cut_slot(i, cut_hi, k, 4), cut_slot(i, cut_lo, k, 4)
            nc.tensor.matmul(dst, l_hi, w_hi, start=start, stop=False)
            nc.tensor.matmul(dst, l_hi, w_lo, start=False, stop=False)
            return nc.tensor.matmul(dst, l_lo, w_hi, start=False, stop=stop)

        def sa_head(n):
            r, g = divmod(n % 8, SAKV)
            return GQ * g + r

        block = ctx.enter_context(nc.Block())

        @block.sync
        def _(sp):
            def load(i):
                if i >= RAW:
                    sp.wait_ge(lo_done, i - RAW + 1)
                for p0, np_, nk, src in slab_source(i):
                    dst = raw[p0:p0 + np_, i % RAW, :].rearrange("p (k c) -> p k c", k=nk)
                    sp.dma_start(dst, src).then_inc(raw_in[i % RAW], 16)

            sp.dma_start(x_tok[:, 0, :], x_d[0:P, :]).then_inc(x_in[0], 16)
            sp.dma_start(gain_rows[0:8, :], norm_mix[0].rearrange("(a b) -> a b", b=P)).then_inc(gains_in, 16)
            sp.dma_start(gain_rows[8:16, :], norm_mlp[0].rearrange("(a b) -> a b", b=P)).then_inc(gains_in, 16)
            for j, g in enumerate((q_norm_sb, k_norm_sb, q_norm_sa, k_norm_sa)):
                sp.dma_start(gain_rows[16 + j:17 + j, :].rearrange("o (a b) -> o a b", b=HD),
                             g.unsqueeze(1).to_broadcast([1, 2, HD])).then_inc(gains_in, 16)
            sp.dma_start(x_tok[:, 1, :], x_d[P:2 * P, :]).then_inc(x_in[1], 16)
            load(0)
            for m in range(2, TB):
                sp.dma_start(x_tok[:, m, :], x_d[m * P:(m + 1) * P, :]).then_inc(x_in[m], 16)
            load(1)
            sp.dma_start(kw_raw, rows(win, 0, 8, C_KW, 40)).then_inc(kw_in, 16)
            for i in range(2, 4):
                load(i)
            sp.wait_ge(kix_zero, 1)
            sp.wait_ge(kix_out, 1)
            for q in range(4):
                sp.dma_start(kz_ix[32 * q:32 * q + 32, q, :], kw_sb[0:IXD, :]).then_inc(kix_rep, 16)
            for i in range(4, SL_BR + 2):
                load(i)
            for i in range(SL_BR + 2, SL_OUT + 4):
                load(i)
            sp.wait_ge(mg_cut, 8)
            sp.dma_start(xres[:, :, :], x_d.rearrange("(m p) c -> p m c", p=P)).then_inc(x2_in, 16)
            for i in range(SL_OUT + 4, SL_END):
                load(i)
            for n in range(2):
                for m in range(TB):
                    sp.wait_ge(f2_out, 8 * (FG - 1) + 4 * n + m + 1)
                    sp.dma_start(out[0, m * P:(m + 1) * P, n * 512:(n + 1) * 512],
                                 xres[:, m, n * 512:(n + 1) * 512]).then_inc(y_out, 16)
            sp.wait_ge(y_out, 16 * 8)

        @block.gpsimd
        def _(pool):
            count = [0]

            def link(ins):
                count[0] += 1
                ins.then_inc(pool_self, 1)
                pool.wait_ge(pool_self, count[0])

            pool.memset(minus_half[:, :], -0.5)
            link(pool.memset(ident[:, :], 0.0))
            pool.affine_select(out=ident[:, :], in_=ident[:, :], compare_op=ALU.not_equal, fill=1.0, base=0,
                               pattern=[[-1, P]], channel_multiplier=1).then_inc(ident_done, 1)
            pool.memset(const_f[:, 0, :], -1.0)
            pool.memset(const_f[:, 1, :], -1.0)
            link(pool.memset(const_f[:, 2, :], 0.0))
            pool.affine_select(out=const_f[:, 0, :], in_=const_f[:, 0, :], compare_op=ALU.is_ge, fill=0.0, base=0,
                               pattern=[[-1, P]], channel_multiplier=1)
            pool.affine_select(out=const_f[:, 2, :], in_=const_f[:, 2, :], compare_op=ALU.is_gt, fill=MASKED, base=0,
                               pattern=[[1, P]], channel_multiplier=-1).then_inc(const_made, 1)
            link(pool.iota(dist_i, pattern=[[-1, S]], base=S - P, channel_multiplier=1))
            pool.tensor_copy(dist[:, :], dist_i).then_inc(dist_done, 1)
            pool.memset(kz_ix, 0.0).then_inc(kix_zero, 1)
            link(pool.memset(topmask[0], 0.0))
            pool.affine_select(out=topmask[0], in_=topmask[0], compare_op=ALU.is_ge, fill=MASKED, base=0,
                               pattern=[[-1, P]], channel_multiplier=1).then_inc(mask0, 1)

            def rows_rsqrt(m):
                pool.wait_ge(row_sq, m + 1)
                link(pool.tensor_scalar(row_ms[:, m:m + 1], row_ss[:, m:m + 1], 1.0 / D, EPS, ALU.mult, ALU.add))
                pool.tensor_tensor(row_r[:, m:m + 1], row_ms[:, m:m + 1], minus_half[:, 0:1],
                                   ALU.pow).then_inc(row_ready, 1)

            def norm_lo(u):
                m, hf = divmod(u, 2)
                at = (slice(None), slice(4 * hf, 4 * hf + 4), slice(m * P, (m + 1) * P))
                pool.wait_ge(nt_hi, u + 1)
                pool.tensor_tensor(a_lo[at], rows_t(u).rearrange("p (a b) -> p a b", a=4), a_hi[at].bitcast(F32),
                                   ALU.subtract).then_inc(nt_cut, 1)

            for m in range(TB):
                rows_rsqrt(m)
                if m >= 1:
                    norm_lo(2 * m - 2)
                    norm_lo(2 * m - 1)
            norm_lo(6)
            norm_lo(7)
            pool.memset(kz_sa[:, :, :], 0.0).then_inc(q_zero, 1)
            pool.memset(qz_sb[:, :, :], 0.0).then_inc(q_zero, 1)
            n_norm = 0
            for g in range(4):
                if g == QSB:
                    for b in range(1, TB):
                        pool.wait_ge(score_done, 8 * b)
                        diag = topmask[b][:, b * P:(b + 1) * P]
                        pool.affine_select(out=diag, in_=diag, compare_op=ALU.is_ge, fill=MASKED, base=0,
                                           pattern=[[-1, P]], channel_multiplier=1).then_inc(causal_done, 1)
                nh = 2 if g == KVI else 8
                for m in range(TB):
                    pool.wait_ge(ss_done, n_norm + 1)
                    j = n_norm % 2
                    link(pool.tensor_scalar(head_ms[:, j, 0:nh], head_ss[:, j, 0:nh], 1.0 / HD, EPS, ALU.mult, ALU.add))
                    pool.tensor_tensor(head_r[:, j, 0:nh], head_ms[:, j, 0:nh], minus_half[:, 0:nh],
                                       ALU.pow).then_inc(hr_done, 1)
                    n_norm += 1

            pool.wait_ge(z_done, 8)
            for n in range(32):
                b, w = n // 8, (n // 8 + 1) * P
                bias = sa_bias[n % 4][:, 0:w]
                if n >= 4:
                    pool.wait_ge(smax_done, n - 3)
                if n % 8 == 0:
                    if b:
                        pool.wait_ge(mask_ready, b)
                    link(pool.tensor_scalar(bias, dist[:, (3 - b) * P:S], -0.5, None, ALU.mult))
                    pool.tensor_tensor(bias, bias, topmask[b], ALU.add).then_inc(bias_done, 1)
                else:
                    pool.wait_ge(bias_done, n)
                    pool.tensor_scalar(bias, sa_bias[(n - 1) % 4][:, 0:w], 2.0 ** (sa_head(n - 1) - sa_head(n)), None,
                                       ALU.mult).then_inc(bias_done, 1)
            for f in range(8):
                pool.wait_ge(br_out, 8 * (f // 4) + 4 + f % 4 + 1)
                pool.tensor_tensor(gates[:, f, :], gates[:, f, :], gates[:, 8 + f, :], ALU.add).then_inc(mg_sum, 1)
            for m in range(TB):
                rows_rsqrt(TB + m)
            for c in range(FF // P):
                pool.wait_ge(f1_hi, c + 1)
                pool.tensor_tensor(a_lo[:, c % KD, :], ff_sq[c % 2], a_hi[:, c % KD, :].bitcast(F32),
                                   ALU.subtract).then_inc(f1_cut, 1)

        @block.scalar
        def _(act):
            A = nc.scalar.activation

            def norm_square(m, src, junk):
                A(junk, src, ACT.Square, accum_out=row_ss[:, m:m + 1]).then_inc(row_sq, 1)

            def norm_hi(u, dst):
                m, hf = divmod(u % 8, 2)
                act.wait_ge(nt_gained, u + 1)
                A(dst[:, 4 * hf:4 * hf + 4, m * P:(m + 1) * P],
                  rows_t(u).rearrange("p (a b) -> p a b", a=4), ACT.Copy).then_inc(nt_hi, 1)

            nc.scalar.preload_act_table_set("natural_log_exp_and_others")
            for m in range(TB):
                act.wait_ge(x_in[m], 16)
                if m >= 1:
                    act.wait_ge(row_sq, m)
                norm_square(m, x_tok[:, m, :], slot(SQ, 2))
                if m == 1:
                    act.wait_ge(gain_t, 1)
                    A(gain[:, :], bank(7, 0, 20), ACT.Copy).then_inc(gain_ready, 1)
                    act_cut(0)
                if m == 2:
                    norm_hi(0, a_hi)
                    norm_hi(1, a_hi)
            act_cut(1)
            for u in range(2, 8):
                norm_hi(u, a_hi)
            for j in (16, 18):
                A(gain[:, j:j + 1], gain[:, j:j + 1], ACT.Copy, scale=HD ** -0.5).then_inc(gain_ready, 1)
            act.wait_ge(kw_in, 16)
            A(kw_hi, kw_raw, ACT.Copy).then_inc(kw_hi_done, 1)

            def square(n):
                g, m = divmod(n, TB)
                act.wait_ge(proj_done, n + 1)
                if n >= 1:
                    act.wait_ge(ss_done, n)
                w = P if g == KVI else S
                A(slot(2)[:, 0:w], bank(m, 0, w), ACT.Square).then_inc(sq_done, 1)

            def turned(n):
                g, m = divmod(n, TB)
                act.wait_ge(tr_done, n + 1)
                b, t = 4 + n % 2, slice(m * P, (m + 1) * P)
                if g == KVI:
                    for q in range(2):
                        p = slice(64 * q, 64 * q + 64)
                        A(kz_sa[p, q, t], bank(b, 0, P)[p, :], ACT.Copy, scale=gain[p, 19:20])
                    A(qixT[0][:, t], bank(b, P, 2 * P), ACT.Copy)
                    A(qixT[1][:, t], bank(b, 2 * P, 3 * P), ACT.Copy).then_inc(tr_out, 1)
                elif g == QSB:
                    for q in range(2):
                        p = slice(64 * q, 64 * q + 64)
                        ins = A(qz_sb[p, q::2, t], bank(b)[p, :].rearrange("p (a b) -> p a b", a=4), ACT.Copy,
                                scale=gain[p, 16:17])
                    ins.then_inc(tr_out, 1)
                else:
                    dst, gj = {KSB: (kT_sb, 17), QSA: (qT_sa, 18)}[g]
                    A(dst[:, :, t], bank(b).rearrange("p (a b) -> p a b", a=4), ACT.Copy,
                      scale=gain[:, gj:gj + 1]).then_inc(tr_out, 1)

            act.wait_ge(gain_ready, 3)
            act.wait_ge(q_zero, 2)
            for g in range(5):
                if g >= 1:
                    for m in range(TB):
                        turned(4 * (g - 1) + m)
                act_cut(2 * g + 2)
                if g == QSB:
                    act.wait_ge(wT_done, 1)
                    A(w_tok[:, :, :], bank(7, 0, TB * IXH).rearrange("p (a b) -> p a b", a=TB), ACT.Copy,
                      scale=IXH ** -0.5).then_inc(w_ready, 1)
                    for u in range(24):
                        w = (u // 8 + 2) * P
                        act.wait_ge(rel_done, u + 1)
                        if u >= 2:
                            act.wait_ge(score_done, u - 1)
                        A(rel[u % 2][:, 0:w], bank(6 + u % 2, 0, w), ACT.Relu, scale=IXD ** -0.5).then_inc(relu_done, 1)
                if g < 4:
                    for m in range(TB):
                        square(4 * g + m)
                act_cut(2 * g + 3)

            def zset(h):
                return ps[:, 3 * (h % 2) * S:3 * (h % 2) * S + ZW]

            def log_part(h):
                act.wait_ge(z_done, h + 1)
                if h >= 2:
                    act.wait_ge(tri_done, h - 1)
                buf = lg[:, h % 2, :]
                A(buf, zset(h), ACT.Abs).then_inc(act_self, 1)
                act.wait_ge(act_self, 2 * h + 1)
                A(buf, buf, ACT.Exp, scale=-1.0).then_inc(act_self, 1)
                act.wait_ge(act_self, 2 * h + 2)
                A(buf, buf, ACT.Ln, bias=1.0).then_inc(ln_done, 1)

            def gate_out(f):
                act.wait_ge(gate_done, f + 1)
                A(gates[:, f, :], bank(7), ACT.Exp, scale=-1.0).then_inc(gate_exp, 1)

            glns = [0]

            def gate_sigmoid(f):
                act.wait_ge(gate_exp, f + 1)
                A(gates[:, f, :], gates[:, f, :], ACT.Ln, bias=1.0).then_inc(gate_ln, 1)
                glns[0] += 1
                act.wait_ge(gate_ln, glns[0])
                A(gates[:, f, :], gates[:, f, :], ACT.Exp, scale=-1.0).then_inc(gsb_ready if f < 8 else gsa_ready, 1)

            log_part(0)
            for h in range(SBH):
                if h % 2 == 0 and h:
                    act_cut(SL_GATE + 1 + h // 2)
                if h < 7:
                    log_part(h + 1)
                act.wait_ge(tri_done, h + 1)
                if h >= 2:
                    act.wait_ge(av_done, h // 2)
                A(weights[h % 2], zset(h), ACT.Exp).then_inc(a_done, 1)
                gate_out(h)
            for n in range(32 + 2):
                if n < 32:
                    w, j = (n // 8 + 1) * P, n % 4
                    act.wait_ge(smax_done, n + 1)
                    A(sa_s[j][:, 0:w], sa_s[j][:, 0:w], ACT.Exp, bias=snmax[:, j:j + 1], scale=-1.0,
                      accum_out=sum_p[:, j:j + 1]).then_inc(p_done, 1)
                if n >= 2:
                    q = n - 2
                    b, u = q // 8, q // 4
                    act.wait_ge(pt_done, q + 1)
                    if u >= 2:
                        act.wait_ge(pv_done, u - 1)
                    A(pT[u % 2][:, q % 2, 0:b + 1, q % 4 // 2, :],
                      bank(2 + q % 2, 0, (b + 1) * P).rearrange("p (a b) -> p a b", b=P), ACT.Copy).then_inc(pt_out, 1)
                    if q % 4 == 3 and q < 31:
                        gate_out(8 + q // 4)
                if n % 8 == 4 and n < 32:
                    act_cut(SL_GATE + 5 + n // 8)
                if n % 4 == 1 and n < 32:
                    gate_sigmoid(n // 4)
                if n % 4 == 3 and n >= 7:
                    gate_sigmoid(7 + n // 4)
            act.wait_ge(pv_done, 8)
            act.wait_ge(pt_out, 32)
            act.wait_ge(osb_out, 4)
            for c in range(8):
                if c == 4:
                    act.wait_ge(osa_out, 8)
                A(b_hi[:, c, :], (oT_sb if c < 4 else qT_sa)[:, c % 4, :], ACT.Copy).then_inc(o_hi, 1)
            gate_out(15)
            gate_sigmoid(15)
            act_cut(SL_BR + 1)
            for q in range(4):
                if q < 4:
                    act_cut(SL_BR + 2 + q)
                if q % 2:
                    for j in range(4):
                        f = 4 * (q // 2) + j
                        act.wait_ge(mg_sum, f + 1)
                        A(a_hi[:, f, :], gates[:, f, :], ACT.Copy).then_inc(mg_hi, 1)
            act_cut(SL_OUT + 2)
            act_cut(SL_OUT + 3)
            act_cut(SL_FF)
            for m in range(TB + 1):
                if m < TB:
                    act.wait_ge(wo_out, 4 + m + 1)
                    act.wait_ge(row_sq, TB + m)
                    norm_square(TB + m, xres[:, m, :], slot(14, 2))
                if m >= 1:
                    norm_hi(8 + 2 * (m - 1), b_hi)
                    norm_hi(9 + 2 * (m - 1), b_hi)
            act_cut(SL_FF + 1)

            def ff1_hidden(c):
                act.wait_ge(f1_done, c + 1)
                A(ff_relu[c % 2], bank(6 + c % 2), ACT.Relu).then_inc(f1_relu, 1)
                act.wait_ge(f1_sq, c + 1)
                A(a_hi[:, c % KD, :], ff_sq[c % 2], ACT.Copy).then_inc(f1_hi, 1)

            for g in range(FG):
                for j in range(8):
                    i = SL_FF + 8 * g + j
                    if j < 4:
                        ff1_hidden(8 * g + 2 * j)
                        ff1_hidden(8 * g + 2 * j + 1)
                    if i + 2 < SL_END:
                        act_cut(i + 2)

        @block.vector
        def _(dve):
            count = [0]

            def link(ins):
                count[0] += 1
                ins.then_inc(dve_self, 1)
                dve.wait_ge(dve_self, count[0])

            V = nc.vector

            dve.wait_ge(ident_done, 1)
            dve.wait_ge(const_made, 1)
            V.tensor_copy(const_r[:, :, :], const_f[:, 0:2, :])
            V.tensor_copy(ident_b, ident[:, :])
            V.tensor_copy(mask_b, mask_f).then_inc(const_cut, 1)

            def norm_scale(m, dst, src):
                dve.wait_ge(row_ready, m + 1)
                V.tensor_scalar(dst, src, row_r[:, m:m + 1], None, ALU.mult).then_inc(row_scaled, 1)

            def norm_gain(u, g0):
                hf = u % 2
                dve.wait_ge(nt_done, u + 1)
                if u >= 2:
                    dve.wait_ge(nt_cut, u - 1)
                V.tensor_tensor(rows_t(u).rearrange("p (a b) -> p a b", a=4),
                                bank(4 + u % 2).rearrange("p (a b) -> p a b", a=4),
                                gain[:, g0 + 4 * hf:g0 + 4 * hf + 4].unsqueeze(2).to_broadcast([P, 4, P]),
                                ALU.mult).then_inc(nt_gained, 1)

            def norm_lo(u, hi, lo):
                m, hf = divmod(u % 8, 2)
                at = (slice(None), slice(4 * hf, 4 * hf + 4), slice(m * P, (m + 1) * P))
                dve.wait_ge(nt_hi, u + 1)
                V.tensor_tensor(lo[at], rows_t(u).rearrange("p (a b) -> p a b", a=4), hi[at].bitcast(F32),
                                ALU.subtract).then_inc(nt_cut, 1)

            for m in range(TB + 1):
                if m < TB:
                    norm_scale(m, x_tok[:, m, :], x_tok[:, m, :])
                if m == 1:
                    dve.wait_ge(gain_ready, 1)
                if m >= 1:
                    norm_gain(2 * m - 2, 0)
                    norm_gain(2 * m - 1, 0)
                if m == 1:
                    dve_cut(0)
                if m == 2:
                    dve_cut(1)
            dve.wait_ge(kw_hi_done, 1)
            V.tensor_tensor(kw_lo, kw_raw, kw_hi.bitcast(F32), ALU.subtract).then_inc(kw_cut, 1)

            def topk_steps():
                for b in range(1, TB):
                    dve.wait_ge(causal_done, b)
                    for r in range(TOPK // 8):
                        link(V.max(best8[:, :], topmask[b]))
                        link(V.match_replace(out=topmask[b], in_to_replace=best8[:, :], in_values=topmask[b],
                                             imm_value=TAKEN))
                        yield
                    V.tensor_scalar(topmask[b], topmask[b], TAKEN * 0.5, MASKED, ALU.is_gt, ALU.mult).then_inc(mask_ready, 1)
                    yield

            steps = topk_steps()

            def topk(n):
                for _ in range(n):
                    next(steps, None)

            def head_sums(n):
                g, m = divmod(n, TB)
                nh = 2 if g == KVI else 8
                dve.wait_ge(sq_done, n + 1)
                if n >= 2:
                    dve.wait_ge(hr_done, n - 1)
                V.tensor_reduce(head_ss[:, n % 2, 0:nh], slot(2)[:, 0:nh * HD].rearrange("p (h d) -> p h d", d=HD),
                                AX.X, ALU.add).then_inc(ss_done, 1)

            def head_scaled(n):
                g, m = divmod(n, TB)
                nh = 2 if g == KVI else 8
                if n >= 2:
                    dve.wait_ge(tr_done, n - 1)
                dve.wait_ge(hr_done, n + 1)
                r = head_r[:, n % 2, 0:nh]
                if g == KVI:
                    V.tensor_copy(v_sa[:, m, :], bank(m, P, 2 * P))
                    V.tensor_copy(tok[n % 2][:, P:3 * P], bank(m, 2 * P, 4 * P))
                if g == QSA:
                    V.tensor_tensor(tok[n % 2].rearrange("p (r g d) -> p g r d", g=2, d=HD),
                                    bank(m).rearrange("p (g r d) -> p g r d", g=2, d=HD),
                                    r.rearrange("p (g r) -> p g r", g=2).unsqueeze(3).to_broadcast([P, 2, 4, HD]),
                                    ALU.mult).then_inc(proj_out, 1)
                else:
                    V.tensor_tensor(tok[n % 2][:, 0:nh * HD].rearrange("p (h d) -> p h d", d=HD),
                                    bank(m, 0, nh * HD).rearrange("p (h d) -> p h d", d=HD),
                                    r.unsqueeze(2).to_broadcast([P, nh, HD]), ALU.mult).then_inc(proj_out, 1)

            for g in range(5):
                dve_cut(2 * g + 2)
                if g == QSB:
                    dve.wait_ge(w_ready, 1)
                    for u in range(24):
                        b, h = u // 8 + 1, u % 8
                        dve.wait_ge(relu_done, u + 1)
                        src, wgt = rel[u % 2][:, 0:(b + 1) * P], w_tok[:, b, h:h + 1]
                        if h == 0:
                            V.tensor_scalar(topmask[b], src, wgt, None, ALU.mult).then_inc(score_done, 1)
                        else:
                            dve.wait_ge(score_done, u)
                            V.scalar_tensor_tensor(out=topmask[b], in0=src, scalar=wgt, in1=topmask[b],
                                                   op0=ALU.mult, op1=ALU.add).then_inc(score_done, 1)
                if g < 4:
                    for m in range(TB):
                        if g == KVI and m == 2:
                            dve.wait_ge(kix_done, 1)
                            V.tensor_copy(kw_sb[0:40, :], bank(6)[0:40, :]).then_inc(kix_out, 1)
                        head_sums(4 * g + m)
                        if g >= KSB:
                            topk(1)
                        head_scaled(4 * g + m)
                else:
                    for m in range(TB):
                        dve.wait_ge(proj_done, 16 + m + 1)
                        V.tensor_copy(v_sb[:, m, :], bank(m)).then_inc(proj_out, 1)
                        topk(1)
                dve_cut(2 * g + 3)
                if g in (KSB, QSA):
                    topk(4)

            def zset(h):
                return ps[:, 3 * (h % 2) * S:3 * (h % 2) * S + ZW]

            def softplus(h):
                buf = lg[:, h % 2, :]
                dve.wait_ge(ln_done, h + 1)
                link(V.scalar_tensor_tensor(out=buf, in0=zset(h), scalar=0.0, in1=buf, op0=ALU.max, op1=ALU.add))
                if h >= 1:
                    dve.wait_ge(tri_done, h)
                link(V.tensor_copy(sp_hi[:, :], buf))
                V.tensor_tensor(sp_lo[:, :], buf, sp_hi[:, :].bitcast(F32), ALU.subtract).then_inc(sp_done, 1)

            def sa_values_out(u):
                b, rp = divmod(u, 2)
                dve.wait_ge(pv_done, u + 1)
                V.tensor_copy(qT_sa[:, 2 * rp:2 * rp + 2, b * P:(b + 1) * P],
                              bank(4 + u % 2, 0, 2 * P).rearrange("p (a b) -> p a b", a=2)).then_inc(osa_out, 1)

            def sa_logits(n):
                w, j = (n // 8 + 1) * P, n % 4
                dve.wait_ge(s_done, n + 1)
                dve.wait_ge(bias_done, n + 1)
                dve.wait_ge(tri_done, 7 if n < 2 else 8)
                if n >= 4:
                    dve.wait_ge(pt_done, n - 3)
                V.tensor_tensor_reduce(out=sa_s[j][:, 0:w], in0=bank(n % 2, 0, w), in1=sa_bias[j][:, 0:w],
                                       scale=-1.0, scalar=3.0e38, op0=ALU.add, op1=ALU.min,
                                       accum_out=snmax[:, j:j + 1]).then_inc(smax_done, 1)

            def pair_out(c):
                dve.wait_ge(av_done, c + 1)
                V.tensor_copy(oT_sb[:, c, :], bank(6)).then_inc(osb_out, 1)

            for h in range(SBH):
                softplus(h)
                if h % 2 == 0 and h:
                    dve_cut(SL_GATE + 1 + h // 2)
                topk(2 if h == 0 else 3)
                if h % 2 == 0 and h:
                    pair_out(h // 2 - 1)
            sa_logits(0)
            sa_logits(1)
            pair_out(3)
            for n in range(2, 32 + 2):
                if n < 32:
                    sa_logits(n)
                q = n - 2
                w, j = (q // 8 + 1) * P, q % 4
                dve.wait_ge(p_done, q + 1)
                link(V.reciprocal(rcp_l[:, j:j + 1], sum_p[:, j:j + 1]))
                V.tensor_scalar(sa_s[j][:, 0:w], sa_s[j][:, 0:w], rcp_l[:, j:j + 1], None, ALU.mult).then_inc(pn_done, 1)
                topk(1 if n < 20 else 60)
                if n % 8 == 5 and n < 32:
                    dve_cut(SL_GATE + 5 + n // 8)
                if n >= 8 and n % 4 == 0:
                    sa_values_out(n // 4 - 2)
            sa_values_out(7)
            for c in range(8):
                dve.wait_ge(o_hi, c + 1)
                V.tensor_tensor(b_lo[:, c, :], (oT_sb if c < 4 else qT_sa)[:, c % 4, :],
                                b_hi[:, c, :].bitcast(F32), ALU.subtract).then_inc(o_cut, 1)
            dve_cut(SL_BR + 1)
            for q in range(4):
                dve_cut(SL_BR + 2 + q)
                dve.wait_ge(*((gsb_ready, 8) if q % 2 == 0 else (gsa_ready, 4 * (q // 2) + 4)))
                for j in range(4):
                    f = 8 * (q % 2) + 4 * (q // 2) + j
                    dve.wait_ge(br_done, 4 * q + j + 1)
                    V.tensor_tensor(gates[:, f, :], bank(4 * (q % 2) + j), gates[:, f, :], ALU.mult).then_inc(br_out, 1)
                if q % 2:
                    for j in range(4):
                        f = 4 * (q // 2) + j
                        dve.wait_ge(mg_hi, f + 1)
                        V.tensor_tensor(a_lo[:, f, :], gates[:, f, :], a_hi[:, f, :].bitcast(F32),
                                        ALU.subtract).then_inc(mg_cut, 1)
            dve.wait_ge(x2_in, 16)

            def add_to_x(n, m):
                part = xres[:, m, n * 512:(n + 1) * 512]
                return V.tensor_tensor(part, bank(m), part, ALU.add)

            dve_cut(SL_OUT + 2)
            for m in range(TB):
                dve.wait_ge(wo_done, m + 1)
                add_to_x(0, m).then_inc(wo_out, 1)
            dve_cut(SL_OUT + 3)
            dve_cut(SL_FF)
            for m in range(TB + 1):
                if m < TB:
                    dve.wait_ge(wo_done, 4 + m + 1)
                    add_to_x(1, m).then_inc(wo_out, 1)
                    norm_scale(TB + m, xn2[m % 2], xres[:, m, :])
                if m >= 1:
                    u = 8 + 2 * m - 2
                    norm_gain(u, 8)
                    norm_gain(u + 1, 8)
                    norm_lo(u, b_hi, b_lo)
                    norm_lo(u + 1, b_hi, b_lo)
            dve_cut(SL_FF + 1)

            def ff1_square(c):
                dve.wait_ge(f1_relu, c + 1)
                if c >= 2:
                    dve.wait_ge(f1_cut, c - 1)
                V.scalar_tensor_tensor(out=ff_sq[c % 2], in0=bank(6 + c % 2), scalar=0.0, in1=ff_relu[c % 2],
                                       op0=ALU.max, op1=ALU.mult).then_inc(f1_sq, 1)

            for g in range(FG):
                for j in range(8):
                    i = SL_FF + 8 * g + j
                    if j < 4:
                        ff1_square(8 * g + 2 * j)
                        ff1_square(8 * g + 2 * j + 1)
                    if j in (5, 7):
                        n = (j - 5) // 2
                        for m in range(TB):
                            dve.wait_ge(f2_done, 8 * g + 4 * n + m + 1)
                            add_to_x(n, m).then_inc(f2_out, 1)
                    if i + 2 < SL_END:
                        dve_cut(i + 2)

        @block.tensor
        def _(pe):
            T = nc.tensor

            def norm_turn(m, src):
                pe.wait_ge(row_scaled, m + 1)
                for hf in range(2):
                    u = 2 * m + hf
                    if u >= 2:
                        pe.wait_ge(nt_gained, u - 1)
                    for k in range(4):
                        t = T.transpose(bank(4 + u % 2, k * P, (k + 1) * P),
                                        src[:, (4 * hf + k) * P:(4 * hf + k + 1) * P], ident[:, :])
                    t.then_inc(nt_done, 1)

            pe.wait_ge(ident_done, 1)
            pe.wait_ge(gains_in, 96)
            T.transpose(bank(7, 0, 20), gain_rows[:, :], ident[0:20, 0:20]).then_inc(gain_t, 1)

            def slab_ready(i):
                pe.wait_ge(lo_done, i + 1)

            def project_part(g, half, m):
                for k in range(4):
                    kk, t = 4 * half + k, slice(m * P, (m + 1) * P)
                    mm = moving_weights(SL_PROJ + 2 * g + half, k, bank(m), a_hi[:, kk, t], a_lo[:, kk, t],
                                        start=(kk == 0), stop=(kk == 7))
                return mm

            def project(g, half):
                slab_ready(SL_PROJ + 2 * g + half)
                for m in range(TB):
                    if half == 0:
                        pe.wait_ge(proj_out, 4 * (g - 1) + m + 1)
                    mm = project_part(g, half, m)
                    if half == 1:
                        mm.then_inc(proj_done, 1)
                    elif m == TB - 1:
                        mm.then_inc(half_done, 1)
                    if half == 0:
                        turn(4 * (g - 1) + m)

            def turn(n):
                g, m = divmod(n, TB)
                pe.wait_ge(proj_out, n + 1)
                if n >= 2:
                    pe.wait_ge(tr_out, n - 1)
                for k in range(3 if g == KVI else 4):
                    t = T.transpose(bank(4 + n % 2, k * P, (k + 1) * P), tok[n % 2][:, k * P:(k + 1) * P], ident[:, :])
                t.then_inc(tr_done, 1)

            norm_turn(0, x_tok[:, 0, :])
            norm_turn(1, x_tok[:, 1, :])
            for m in range(TB):
                pe.wait_ge(nt_cut, 2 * m + 2)
                if m == 0:
                    slab_ready(0)
                project_part(KVI, 0, m)
                if m == 0:
                    slab_ready(1)
                if 1 <= m < 3:
                    norm_turn(m + 1, x_tok[:, m + 1, :])
                project_part(KVI, 1, m).then_inc(proj_done, 1)
            pe.wait_ge(kw_cut, 1)
            for k in range(KD):
                T.matmul(bank(6)[0:40, :], kw_hi[:, k, :], a_hi[:, k, :], start=(k == 0), stop=False)
                T.matmul(bank(6)[0:40, :], kw_hi[:, k, :], a_lo[:, k, :], start=False, stop=False)
                mm = T.matmul(bank(6)[0:40, :], kw_lo[:, k, :], a_hi[:, k, :], start=False, stop=(k == KD - 1))
            mm.then_inc(kix_done, 1)

            def indexer():
                pe.wait_ge(kix_out, 1)
                for m in range(TB):
                    t = T.transpose(bank(7, m * IXH, (m + 1) * IXH), kw_sb[32:40, m * P:(m + 1) * P], ident[32:40, 32:40])
                t.then_inc(wT_done, 1)
                pe.wait_ge(tr_out, 4)
                pe.wait_ge(kix_rep, 64)
                pe.wait_ge(w_ready, 1)
                for u in range(24):
                    b, h = u // 8 + 1, u % 8
                    if u >= 2:
                        pe.wait_ge(relu_done, u - 1)
                    T.matmul(bank(6 + u % 2, 0, (b + 1) * P), qixT[h // 4][:, b * P:(b + 1) * P],
                             kz_ix[:, h % 4, 0:(b + 1) * P], start=True, stop=True).then_inc(rel_done, 1)

            for g in range(1, 5):
                project(g, 0)
                if g == QSB:
                    indexer()
                project(g, 1)

            def zt(h, i, t0=None):
                t0 = i if t0 is None else t0
                a = 3 * (h % 2) * S + ZCOL[i]
                return ps[:, a + (t0 - i) * P:a + (4 - i) * P]

            def logits(h):
                c = h // 2
                if h >= 2:
                    pe.wait_ge(a_done, h - 1)
                for i in range(4):
                    T.matmul(zt(h, i), kT_sb[:, c, i * P:(i + 1) * P], qz_sb[:, h, i * P:S],
                             start=(i != 3), stop=False, skip_group_check=True)
                    mm = T.matmul(zt(h, i)[:, 0:P], ident_b, mask_b, start=False, stop=False, skip_group_check=True)
                mm.then_inc(z_done, 1)

            def sum_later(h):
                pe.wait_ge(sp_done, h + 1)
                for i in range(4):
                    for j in range(i, 4):
                        a = ZCOL[j]
                        if j == 3:
                            mm = T.matmul(zt(h, i, j), tri_f if i == j else ones_f, lg[:, h % 2, a:a + P],
                                          start=False, stop=True, skip_group_check=True)
                            continue
                        for part in (sp_hi, sp_lo):
                            mm = T.matmul(zt(h, i, j), tri_r if i == j else ones_r, part[:, a:a + (4 - j) * P],
                                          start=False, stop=False, skip_group_check=True)
                mm.then_inc(tri_done, 1)

            def weighted_values(c):
                pe.wait_ge(a_done, 2 * c + 2)
                if c >= 1:
                    pe.wait_ge(osb_out, c)
                for i in range(4):
                    for h in (2 * c, 2 * c + 1):
                        p0 = 64 * (h % 2)
                        mm = T.matmul(bank(6, i * P, S)[p0:p0 + 64, :], v_sb[:, i, h * HD:(h + 1) * HD],
                                      weights[h % 2][:, ZCOL[i]:ZCOL[i] + (4 - i) * P], start=(i == 0), stop=(i == 3),
                                      skip_group_check=True)
                mm.then_inc(av_done, 1)

            def gate(f, k0=0, k1=KD):
                i = SL_GATE + f // 2
                if k0 == 0:
                    slab_ready(i)
                    if f >= 1:
                        pe.wait_ge(gate_exp, f)
                for k in range(k0, k1):
                    mm = stationary_weights(i, k, KD, (f % 2) * P, bank(7), a_hi[:, k, :], a_lo[:, k, :],
                                            start=(k == 0), stop=(k == KD - 1))
                if k1 == KD:
                    mm.then_inc(gate_done, 1)

            def sa_scores(n):
                b = n // 8
                r, g = divmod(n % 8, SAKV)
                if n >= 2:
                    pe.wait_ge(smax_done, n - 1)
                T.matmul(bank(n % 2, 0, (b + 1) * P), qT_sa[:, r, b * P:(b + 1) * P],
                         kz_sa[:, g, 0:(b + 1) * P], start=True, stop=True).then_inc(s_done, 1)

            pe.wait_ge(const_cut, 1)
            pe.wait_ge(tr_out, 16)
            pe.wait_ge(proj_out, 20)
            pe.wait_ge(score_done, 24)
            logits(0)
            for h in range(SBH):
                if h < 7:
                    logits(h + 1)
                gate(h, 0, 4 if h else 8)
                if h == 7:
                    sa_scores(0)
                    sa_scores(1)
                sum_later(h)
                if h:
                    gate(h, 4, 8)
                if h % 2:
                    weighted_values(h // 2)

            def sa_turn(n):
                b = n // 8
                pe.wait_ge(pn_done, n + 1)
                if n >= 2:
                    pe.wait_ge(pt_out, n - 1)
                for i in range(b + 1):
                    t = T.transpose(bank(2 + n % 2, i * P, (i + 1) * P), sa_s[n % 4][:, i * P:(i + 1) * P], ident[:, :])
                t.then_inc(pt_done, 1)

            def sa_values(u):
                b = u // 2
                pe.wait_ge(pt_out, 4 * u + 4)
                if u >= 2:
                    pe.wait_ge(osa_out, u - 1)
                for i in range(b + 1):
                    for g in range(SAKV):
                        mm = T.matmul(bank(4 + u % 2, 0, 2 * P)[64 * g:64 * g + 64, :], v_sa[:, i, 64 * g:64 * g + 64],
                                      pT[u % 2][:, g, i], start=(i == 0), stop=(i == b))
                mm.then_inc(pv_done, 1)

            pe.wait_ge(a_done, 8)
            sa_scores(2)
            for n in range(32):
                sa_turn(n)
                if n < 29:
                    sa_scores(n + 3)
                if n < 28:
                    gate(8 + n // 4, 2 * (n % 4), 2 * (n % 4) + 2)
                if n >= 4 and n % 4 == 0:
                    sa_values(n // 4 - 1)
            sa_values(7)
            gate(15)

            pe.wait_ge(osa_out, 8)
            for q in range(4):
                i = SL_BR + q
                slab_ready(i)
                for j in range(4):
                    if q == 1 and j == 3:
                        pe.wait_ge(gate_exp, 16)
                    if q >= 2:
                        pe.wait_ge(br_out, 4 * (q - 2) + j + 1)
                    for k in range(4):
                        c = 4 * (q % 2) + k
                        if q < 2 and j == 0:
                            pe.wait_ge(o_cut, c + 1)
                        mm = stationary_weights(i, k, 4, j * P, bank(4 * (q % 2) + j), b_hi[:, c, :], b_lo[:, c, :],
                                                start=(k == 0), stop=(k == 3))
                    mm.then_inc(br_done, 1)

            def out_part(n, half, m):
                for k in range(4):
                    kk, t = 4 * half + k, slice(m * P, (m + 1) * P)
                    if n == 0 and m == 0:
                        pe.wait_ge(mg_cut, kk + 1)
                    mm = moving_weights(SL_OUT + 2 * n + half, k, bank(m), a_hi[:, kk, t], a_lo[:, kk, t],
                                        start=(kk == 0), stop=(kk == 7))
                return mm

            slab_ready(SL_OUT)
            pe.wait_ge(br_out, 12)
            for m in range(TB):
                mm = out_part(0, 0, m)
            mm.then_inc(half_done, 1)
            slab_ready(SL_OUT + 1)
            for m in range(TB):
                out_part(0, 1, m).then_inc(wo_done, 1)
            for m in range(2):
                pe.wait_ge(wo_out, m + 1)
                out_part(1, 0, m)
            slab_ready(SL_OUT + 3)
            for m in range(TB):
                if m >= 2:
                    pe.wait_ge(wo_out, m + 1)
                    out_part(1, 0, m)
                out_part(1, 1, m).then_inc(wo_done, 1)
                if m >= 1:
                    norm_turn(TB + m - 1, xn2[(m - 1) % 2])

            def ff1_part(c, t0, t1):
                for k in range(KD):
                    mm = stationary_weights(SL_FF + 8 * (c // 8) + c % 8 // 2, k, KD, (c % 2) * P,
                                            bank(6 + c % 2, t0, t1), b_hi[:, k, t0:t1], b_lo[:, k, t0:t1],
                                            start=(k == 0), stop=(k == KD - 1))
                return mm

            slab_ready(SL_FF)
            pe.wait_ge(nt_cut, 12)
            ff1_part(0, 0, 256)
            ff1_part(1, 0, 256)
            norm_turn(TB + 3, xn2[1])

            pe.wait_ge(nt_cut, 16)
            for g in range(FG):
                for j in range(4):
                    i = SL_FF + 8 * g + j
                    slab_ready(i)
                    for o in range(2):
                        c = 8 * g + 2 * j + o
                        if c >= 2:
                            pe.wait_ge(f1_sq, c - 1)
                        ff1_part(c, 0 if c >= 2 else 256, S).then_inc(f1_done, 1)
                for q in range(4):
                    n, half = divmod(q, 2)
                    i = SL_FF + 8 * g + 4 + q
                    slab_ready(i)
                    for m in range(TB):
                        e = 8 * g + 4 * n + m
                        if half == 0:
                            if e >= 4:
                                pe.wait_ge(f2_out, e - 3)
                            else:
                                pe.wait_ge(wo_out, 5 + m)
                        for k in range(4):
                            kk, t = 4 * half + k, slice(m * P, (m + 1) * P)
                            if n == 0 and m == 0:
                                pe.wait_ge(f1_cut, 8 * g + kk + 1)
                            mm = moving_weights(i, k, bank(m), a_hi[:, kk, t], a_lo[:, kk, t],
                                                start=(kk == 0), stop=(kk == 7))
                        if half == 1:
                            mm.then_inc(f2_done, 1)
                    if half == 0:
                        mm.then_inc(half_done, 1)


_INS = ["x", "norm_mix", "w_in", "q_norm_sb", "k_norm_sb", "q_norm_sa", "k_norm_sa",
        "w_branch_sb", "w_branch_sa", "w_out", "norm_mlp", "w_ff1", "w_ff2"]
_OUTS = [((1, S, D), "float32")]


def kernel(**inputs):
    import numpy as _np
    import concourse.bacc as _bacc
    from concourse import mybir as _mybir
    from concourse.bass_utils import run_bass_kernel_spmd as _run

    nc = _bacc.Bacc("TRN2", target_bir_lowering=False, num_devices=1)
    arrays, args = {}, []
    for name in _INS:
        a = _np.ascontiguousarray(inputs[name])
        arrays[f"in_{name}_dram"] = a
        args.append(nc.dram_tensor(f"in_{name}_dram", a.shape, _mybir.dt.from_np(a.dtype), kind="ExternalInput").ap())
    for i, (shape, dtype) in enumerate(_OUTS):
        dt = _mybir.dt.from_np(_np.dtype(dtype))
        args.append(nc.dram_tensor(f"out_{i}_dram", shape, dt, kind="ExternalOutput").ap())
    block_kernel(nc, *args)
    r = _run(nc, [arrays], core_ids=[0])
    got = tuple(r.results[0][f"out_{i}_dram"] for i in range(len(_OUTS)))
    return got[0]
```

```python
from contextlib import ExitStack

import concourse.bass as bass
from concourse import mybir

ALU = mybir.AluOpType
ACT = mybir.ActivationFunctionType
AX = mybir.AxisListType
F32 = mybir.dt.float32
F32R = mybir.dt.float32r
I32 = mybir.dt.int32
BF16 = mybir.dt.bfloat16

P = 128
S = 512
D = 1024
FF = 4 * D
TB = S // P
KD = D // P
HD = 64
SBH = 8
SAH, SAKV = 8, 2
GQ = SAH // SAKV
IXH, IXD = 8, 32
TOPK = min(256, S // 4)
EPS = 1e-6
MASKED = -1e30
TAKEN = -3e38

C_QSB, C_KSB, C_VSB, C_QSA, C_KVI = 0, 512, 1024, 1536, 2048
C_KW = 2560
C_GATE = 2600

RAW, CUT, SLAB = 4, 2, 2048

GROUPS = [C_KVI, C_QSB, C_KSB, C_QSA, C_VSB]
KVI, QSB, KSB, QSA, VSB = range(5)
SL_PROJ = 0
SL_GATE = SL_PROJ + 2 * len(GROUPS)
SL_BR = SL_GATE + 8
SL_OUT = SL_BR + 4
SL_FF = SL_OUT + 4
FG = 4
SL_END = SL_FF + 8 * FG

ZCOL = [0, 512, 1024, 896]
ZW = 1280
WARM = (8, 27)


def block_kernel(nc, x, norm_mix, w_in, q_norm_sb, k_norm_sb, q_norm_sa, k_norm_sa,
                 w_branch_sb, w_branch_sa, w_out, norm_mlp, w_ff1, w_ff2, out):
    ctx = ExitStack()
    with ctx:
        def sb(name, shape, dt, where=ctx):
            return where.enter_context(nc.sbuf_tensor(name, shape, dt))

        def sem(name):
            return ctx.enter_context(nc.semaphore(name))

        raw = sb("raw", [P, RAW, SLAB], F32)
        cut_hi = sb("cut_hi", [P, CUT, SLAB], F32R)
        cut_lo = sb("cut_lo", [P, CUT, SLAB], F32R)
        a_hi = sb("a_hi", [P, KD, S], F32R)
        a_lo = sb("a_lo", [P, KD, S], F32R)
        stacks = ExitStack()
        sb("below_k_stack", [P, 5, S], F32, stacks)
        k_stack = sb("k_stack", [P, S], F32R, stacks)
        sb("below_q_stack", [P, 2, S], F32, stacks)
        q_stack = sb("q_stack", [P, IXH, S], F32R, stacks)
        stacks.close()
        gates = sb("gates", [P, 16, S], F32)
        qz_sb = sb("qz_sb", [P, SBH, S], F32)
        oT_sb = qz_sb[:, 0::2, :]
        qT_sa = sb("qT_sa", [P, 4, S], F32)
        ident = sb("ident", [P, P], F32)
        const_f = sb("const_f", [P, 3, P], F32)
        tri_f, ones_f, mask_f = (const_f[:, j, :] for j in range(3))
        const_r = sb("const_r", [P, 2, P], F32R)
        tri_r, ones_r = const_r[:, 0, :], const_r[:, 1, :]
        const_b = sb("const_b", [P, 2, P], BF16)
        ident_b, mask_b = const_b[:, 0, :], const_b[:, 1, :]
        cold_b = sb("cold_b", [P, S], BF16)
        dist = sb("dist", [P, S], F32)
        dist_i = dist[:, :].bitcast(I32)
        gain = sb("gain", [P, 20], F32)
        w_tok = sb("w_tok", [P, TB, IXH], F32)
        row_ss = sb("row_ss", [P, 2 * TB], F32)
        row_ms = sb("row_ms", [P, 2 * TB], F32)
        row_r = sb("row_r", [P, 2 * TB], F32)
        head_ss = sb("head_ss", [P, 2, 8], F32)
        head_ms = sb("head_ms", [P, 2, 8], F32)
        head_r = sb("head_r", [P, 2, 8], F32)
        minus_half = sb("minus_half", [P, 8], F32)
        best8 = sb("best8", [P, 8], F32)
        snmax = sb("snmax", [P, 4], F32)
        sum_p = sb("sum_p", [P, 4], F32)
        rcp_l = sb("rcp_l", [P, 4], F32)

        early = ExitStack()
        kv_sb = sb("kv_sb", [P, 2, 4, S], F32, early)
        kT_sb, v_sb = kv_sb[:, 0], kv_sb[:, 1]
        kz_sa = sb("kz_sa", [P, SAKV, S], F32, early)
        v_sa = sb("v_sa", [P, TB, P], F32, early)
        lg = sb("lg", [P, 2, ZW], F32, early)
        sp_hi = sb("sp_hi", [P, ZW], F32R, early)
        sp_lo = sb("sp_lo", [P, ZW], F32R, early)
        topm = sb("topm", [P, ZW], F32, early)
        early.close()
        late = ExitStack()
        b_hi = sb("b_hi", [P, KD, S], F32R, late)
        b_lo = sb("b_lo", [P, KD, S], F32R, late)
        cut3_hi = sb("cut3_hi", [P, SLAB], F32R, late)
        cut3_lo = sb("cut3_lo", [P, SLAB], F32R, late)
        late.close()

        def slot(j, n=1):
            return gates[:, j:j + n, :].rearrange("p a b -> p (a b)")
        x_tok = gates[:, 0:8, :].rearrange("p (m a) b -> p m (a b)", m=TB)
        xres = x_tok
        SQ = 8

        def rows_t(u):
            return slot((10 if u < 8 else 12) + u % 2)
        xn2 = [slot(8, 2), slot(10, 2)]
        ff_sq, ff_relu = [slot(12), slot(13)], [slot(14), slot(15)]
        tok = [slot(0), slot(1)]
        kw_sb = slot(6)
        lg_flat = lg[:, :, :].rearrange("p a b -> p (a b)")
        q_parts = [t[:, 0:2 * S].rearrange("p (a b) -> p a b", a=2) for t in (sp_hi, sp_lo)]
        k_parts = [slot(3).bitcast(F32R), slot(4).bitcast(F32R)]
        q_in, k_in = gates[:, 8:16, :], slot(5)
        kw_raw = lg[:, 0, 0:320].rearrange("p (k c) -> p k c", k=KD)
        gain_rows = lg[0:20, 0, 384:512]
        kw_hi, kw_lo = (t[:, 0:320].rearrange("p (k c) -> p k c", k=KD) for t in (sp_hi, sp_lo))
        rel = [lg_flat[:, j * S:(j + 1) * S] for j in range(2)]
        MOFF = [0, 128, 384, 768]
        topmask = [topm[:, MOFF[b]:MOFF[b] + (b + 1) * P] for b in range(TB)]
        weights = [gates[:, a:a + 3, :].rearrange("p a b -> p (a b)")[:, 0:ZW] for a in (8, 11)]
        sa_s = [lg_flat[:, j * S:(j + 1) * S] for j in range(4)]
        sa_bias = [qz_sb[:, 2 * j + 1, :] for j in range(4)]
        pT = [kv_sb[:, j].rearrange("p a b -> p (a b)").rearrange("p (g i r t) -> p g i r t", g=SAKV, i=4, r=2)
              for j in range(2)]

        ps = ctx.enter_context(nc.psum_tensor("ps", [P, 8 * S], F32))

        def bank(j, a=0, b=S):
            return ps[:, j * S + a:j * S + b]

        x_in = [sem(f"x_in{m}") for m in range(TB)]
        x2_in = [sem(f"x2_in{m}") for m in range(TB)]
        gains_in, kw_in = sem("gains_in"), sem("kw_in")
        raw_in = [sem(f"raw_in{j}") for j in range(RAW)]
        hi_done, lo_done, half_done = sem("hi_done"), sem("lo_done"), sem("half_done")
        pool_self, dve_self, act_self = sem("pool_self"), sem("dve_self"), sem("act_self")
        ident_done, const_made, const_cut, dist_done = sem("ident_done"), sem("const_made"), sem("const_cut"), sem("dist_done")
        gain_t, gain_ready = sem("gain_t"), sem("gain_ready")
        kw_hi_done, kw_cut = sem("kw_hi_done"), sem("kw_cut")
        row_sq, row_ready, row_scaled = sem("row_sq"), sem("row_ready"), sem("row_scaled")
        nt_done, nt_gained, nt_hi, nt_cut = sem("nt_done"), sem("nt_gained"), sem("nt_hi"), sem("nt_cut")
        proj_done, sq_done, ss_done, hr_done = sem("proj_done"), sem("sq_done"), sem("ss_done"), sem("hr_done")
        proj_out, tr_done, tr_out = sem("proj_out"), sem("tr_done"), sem("tr_out")
        kix_done, kix_out, ix_stacked, wT_done, w_ready = sem("kix_done"), sem("kix_out"), sem("ix_stacked"), sem("wT_done"), sem("w_ready")
        rel_done, relu_done, score_done, causal_done, mask_ready, q_zero, qix_hi, ix_ready = sem("rel_done"), sem("relu_done"), sem("score_done"), sem("causal_done"), sem("mask_ready"), sem("q_zero"), sem("qix_hi"), sem("ix_ready")
        mask0 = sem("mask0")
        z_done, ln_done, sp_done, tri_done, a_done, av_done, osb_out = (sem(n) for n in (
            "z_done", "ln_done", "sp_done", "tri_done", "a_done", "av_done", "osb_out"))
        gate_done, gate_exp, gate_ln, gsb_ready, gsa_ready = (sem(n) for n in (
            "gate_done", "gate_exp", "gate_ln", "gsb_ready", "gsa_ready"))
        bias_done, s_done, smax_done, p_done, pn_done, pt_done, pt_out, pv_done, osa_out = (
            sem(n) for n in ("bias_done", "s_done", "smax_done", "p_done", "pn_done",
                             "pt_done", "pt_out", "pv_done", "osa_out"))
        o_hi, o_cut = sem("o_hi"), sem("o_cut")
        br_done, br_out, mg_sum, mg_hi, mg_cut = (sem(n) for n in ("br_done", "br_out", "mg_sum", "mg_hi", "mg_cut"))
        wo_done, wo_out = sem("wo_done"), sem("wo_out")
        f1_done, f1_relu, f1_sq, f1_hi, f1_cut = (sem(n) for n in ("f1_done", "f1_relu", "f1_sq", "f1_hi", "f1_cut"))
        f2_done, f2_out, y_out = sem("f2_done"), sem("f2_out"), sem("y_out")

        def rows(w, r0, nk, c0, nc_):
            return w[r0:r0 + nk * P, c0:c0 + nc_].rearrange("(k p) c -> p k c", p=P)

        x_d = x[0]
        win, wsb, wsa, wout, wf1, wf2 = w_in[0], w_branch_sb[0], w_branch_sa[0], w_out[0], w_ff1[0], w_ff2[0]

        def slab_source(i):
            if i < SL_GATE:
                g, half = divmod(i - SL_PROJ, 2)
                return [(0, P, 4, rows(win, half * 512, 4, GROUPS[g], 512))]
            if i < SL_BR:
                return [(0, P, 8, rows(win, 0, 8, C_GATE + 256 * (i - SL_GATE), 256))]
            if i < SL_OUT:
                q = i - SL_BR
                c0 = 512 * (q // 2)
                if q % 2 == 0:
                    return [(0, P, 4, rows(wsb, 0, 4, c0, 512))]
                return [(64 * g, 64, 4, wsa[256 * g:256 * g + 256, c0:c0 + 512].rearrange("(r d) c -> d r c", d=HD))
                        for g in range(SAKV)]
            if i < SL_FF:
                n, half = divmod(i - SL_OUT, 2)
                return [(0, P, 4, rows(wout, half * 512, 4, n * 512, 512))]
            g, j = divmod(i - SL_FF, 8)
            if j < 4:
                return [(0, P, 8, rows(wf1, 0, 8, 1024 * g + 256 * j, 256))]
            n, half = divmod(j - 4, 2)
            return [(0, P, 4, rows(wf2, 1024 * g + half * 512, 4, n * 512, 512))]

        def slab_arrived(i):
            n = sum(len(slab_source(j)) for j in range(i % RAW, i + 1, RAW))
            return raw_in[i % RAW], 16 * n

        def slab_used(i):
            if i < SL_GATE:
                g, half = divmod(i - SL_PROJ, 2)
                return (proj_done, 4 * g + 4) if half or g == 0 else (half_done, g)
            if i < SL_BR:
                return gate_done, 2 * (i - SL_GATE) + 2
            if i < SL_OUT:
                return br_done, 4 * (i - SL_BR) + 4
            if i < SL_FF:
                n, half = divmod(i - SL_OUT, 2)
                return (wo_done, 4 * n + 4) if half or n == 1 else (half_done, len(GROUPS))
            g, j = divmod(i - SL_FF, 8)
            if j < 4:
                return f1_done, 8 * g + 2 * j + 2
            n, half = divmod(j - 4, 2)
            return (f2_done, 8 * g + 4 * n + 4) if half else (half_done, len(GROUPS) + 2 * g + n + 1)

        def cut_slot(i, part, k, nk):
            w = SLAB // nk
            slab = part[:, i % CUT, :]
            if i == SL_FF:
                slab = cut3_hi if part is cut_hi else cut3_lo
            return slab[:, k * w:(k + 1) * w]

        def act_cut(i, part=0, parts=1):
            if part == 0:
                nc.scalar.wait_ge(*slab_arrived(i))
                if i >= CUT and i != SL_FF:
                    nc.scalar.wait_ge(*slab_used(i - CUT))
            w = SLAB // parts
            cut = nc.scalar.activation(cut_slot(i, cut_hi, part, parts), raw[:, i % RAW, part * w:(part + 1) * w], ACT.Copy)
            if part == parts - 1:
                cut.then_inc(hi_done, 1)

        def dve_cut(i, part=0, parts=1):
            nc.vector.wait_ge(hi_done, i + 1)
            w = SLAB // parts
            cut = nc.vector.tensor_tensor(cut_slot(i, cut_lo, part, parts), raw[:, i % RAW, part * w:(part + 1) * w],
                                          cut_slot(i, cut_hi, part, parts).bitcast(F32), ALU.subtract)
            if part == parts - 1:
                cut.then_inc(lo_done, 1)

        def stationary_weights(i, k, nk, col, dst, rhs_hi, rhs_lo, start, stop):
            w_hi = cut_slot(i, cut_hi, k, nk)[:, col:col + P]
            w_lo = cut_slot(i, cut_lo, k, nk)[:, col:col + P]
            nc.tensor.matmul(dst, w_hi, rhs_hi, start=start, stop=False)
            nc.tensor.matmul(dst, w_hi, rhs_lo, start=False, stop=False)
            return nc.tensor.matmul(dst, w_lo, rhs_hi, start=False, stop=stop)

        def moving_weights(i, k, dst, l_hi, l_lo, start, stop):
            w_hi, w_lo = cut_slot(i, cut_hi, k, 4), cut_slot(i, cut_lo, k, 4)
            nc.tensor.matmul(dst, l_hi, w_hi, start=start, stop=False)
            nc.tensor.matmul(dst, l_hi, w_lo, start=False, stop=False)
            return nc.tensor.matmul(dst, l_lo, w_hi, start=False, stop=stop)

        def sa_head(n):
            r, g = divmod(n % 8, SAKV)
            return GQ * g + r

        block = ctx.enter_context(nc.Block())

        @block.sync
        def _(sp):
            def load(i):
                if i >= RAW:
                    sp.wait_ge(lo_done, i - RAW + 1)
                for p0, np_, nk, src in slab_source(i):
                    dst = raw[p0:p0 + np_, i % RAW, :].rearrange("p (k c) -> p k c", k=nk)
                    sp.dma_start(dst, src).then_inc(raw_in[i % RAW], 16)

            sp.dma_start(x_tok[:, 0, :], x_d[0:P, :]).then_inc(x_in[0], 16)
            sp.dma_start(gain_rows[0:8, :], norm_mix[0].rearrange("(a b) -> a b", b=P)).then_inc(gains_in, 16)
            sp.dma_start(gain_rows[8:16, :], norm_mlp[0].rearrange("(a b) -> a b", b=P)).then_inc(gains_in, 16)
            for j, g in enumerate((q_norm_sb, k_norm_sb, q_norm_sa, k_norm_sa)):
                sp.dma_start(gain_rows[16 + j:17 + j, :].rearrange("o (a b) -> o a b", b=HD),
                             g.unsqueeze(1).to_broadcast([1, 2, HD])).then_inc(gains_in, 16)
            load(0)
            sp.dma_start(x_tok[:, 1, :], x_d[P:2 * P, :]).then_inc(x_in[1], 16)
            load(1)
            for m in range(2, TB):
                sp.dma_start(x_tok[:, m, :], x_d[m * P:(m + 1) * P, :]).then_inc(x_in[m], 16)
            sp.dma_start(kw_raw, rows(win, 0, 8, C_KW, 40)).then_inc(kw_in, 16)
            for i in range(2, 6):
                load(i)
            sp.wait_ge(kix_out, 1)
            for quad in range(4):
                p = slice(IXD * quad, IXD * quad + IXD)
                sp.dma_start(k_in[p, :], k_parts[quad % 2][0:IXD, :].bitcast(F32)).then_inc(ix_stacked, 16)
            sp.wait_ge(tr_out, 4)
            for quad in range(4):
                p = slice(IXD * quad, IXD * quad + IXD)
                for h in range(4):
                    sp.dma_start(q_in[p, h::4, :],
                                 q_parts[quad // 2][IXD * h:IXD * h + IXD, :, :].bitcast(F32)).then_inc(ix_stacked, 16)
            for i in range(6, SL_OUT + 4):
                load(i)
            for m in range(TB):
                sp.wait_ge(mg_cut, 4 * (m // 2) + 4)
                sp.dma_start(xres[:, m, :], x_d[m * P:(m + 1) * P, :]).then_inc(x2_in[m], 16)
            for i in range(SL_OUT + 4, SL_END):
                load(i)
            for n in range(2):
                for m in range(TB):
                    sp.wait_ge(f2_out, 8 * (FG - 1) + 4 * n + m + 1)
                    sp.dma_start(out[0, m * P:(m + 1) * P, n * 512:(n + 1) * 512],
                                 xres[:, m, n * 512:(n + 1) * 512]).then_inc(y_out, 16)
            sp.wait_ge(y_out, 16 * 8)

        @block.gpsimd
        def _(pool):
            count = [0]

            def link(ins):
                count[0] += 1
                ins.then_inc(pool_self, 1)
                pool.wait_ge(pool_self, count[0])

            pool.memset(minus_half[:, :], -0.5)
            link(pool.memset(ident[:, :], 0.0))
            pool.affine_select(out=ident[:, :], in_=ident[:, :], compare_op=ALU.not_equal, fill=1.0, base=0,
                               pattern=[[-1, P]], channel_multiplier=1).then_inc(ident_done, 1)
            pool.memset(const_f[:, 0, :], -1.0)
            pool.memset(const_f[:, 1, :], -1.0)
            link(pool.memset(const_f[:, 2, :], 0.0))
            pool.affine_select(out=const_f[:, 0, :], in_=const_f[:, 0, :], compare_op=ALU.is_ge, fill=0.0, base=0,
                               pattern=[[-1, P]], channel_multiplier=1)
            pool.affine_select(out=const_f[:, 2, :], in_=const_f[:, 2, :], compare_op=ALU.is_gt, fill=MASKED, base=0,
                               pattern=[[1, P]], channel_multiplier=-1).then_inc(const_made, 1)

            def rows_rsqrt(m):
                pool.wait_ge(row_sq, m + 1)
                link(pool.tensor_scalar(row_ms[:, m:m + 1], row_ss[:, m:m + 1], 1.0 / D, EPS, ALU.mult, ALU.add))
                pool.tensor_tensor(row_r[:, m:m + 1], row_ms[:, m:m + 1], minus_half[:, 0:1],
                                   ALU.pow).then_inc(row_ready, 1)

            for m in range(TB):
                rows_rsqrt(m)
            n_norm = 0
            for g in range(4):
                nh = 2 if g == KVI else 8
                for m in range(TB):
                    if g == KVI and m == 2:
                        pool.memset(kz_sa[:, :, :], 0.0).then_inc(q_zero, 1)
                    if g == KSB and m != 2:
                        b = (1, 2, None, 3)[m]
                        pool.wait_ge(score_done, 8 * b)
                        diag = topmask[b][:, b * P:(b + 1) * P]
                        pool.affine_select(out=diag, in_=diag, compare_op=ALU.is_ge, fill=MASKED, base=0,
                                           pattern=[[-1, P]], channel_multiplier=1).then_inc(causal_done, 1)
                    pool.wait_ge(ss_done, n_norm + 1)
                    j = n_norm % 2
                    link(pool.tensor_scalar(head_ms[:, j, 0:nh], head_ss[:, j, 0:nh], 1.0 / HD, EPS, ALU.mult, ALU.add))
                    pool.tensor_tensor(head_r[:, j, 0:nh], head_ms[:, j, 0:nh], minus_half[:, 0:nh],
                                       ALU.pow).then_inc(hr_done, 1)
                    n_norm += 1
                if g == KVI:
                    pool.memset(qz_sb[:, :, :], 0.0).then_inc(q_zero, 1)
                if g == QSB:
                    link(pool.iota(dist_i, pattern=[[-1, S]], base=S - P, channel_multiplier=1))
                    pool.tensor_copy(dist[:, :], dist_i).then_inc(dist_done, 1)
                    link(pool.memset(topmask[0], 0.0))
                    pool.affine_select(out=topmask[0], in_=topmask[0], compare_op=ALU.is_ge, fill=MASKED, base=0,
                                       pattern=[[-1, P]], channel_multiplier=1).then_inc(mask0, 1)

            pool.wait_ge(z_done, 8)
            for n in range(32):
                b, w = n // 8, (n // 8 + 1) * P
                bias = sa_bias[n % 4][:, 0:w]
                if n >= 4:
                    pool.wait_ge(smax_done, n - 3)
                if n % 8 == 0:
                    if b:
                        pool.wait_ge(mask_ready, b)
                    link(pool.tensor_scalar(bias, dist[:, (3 - b) * P:S], -0.5, None, ALU.mult))
                    pool.tensor_tensor(bias, bias, topmask[b], ALU.add).then_inc(bias_done, 1)
                else:
                    pool.wait_ge(bias_done, n)
                    pool.tensor_scalar(bias, sa_bias[(n - 1) % 4][:, 0:w], 2.0 ** (sa_head(n - 1) - sa_head(n)), None,
                                       ALU.mult).then_inc(bias_done, 1)
            for f in range(8):
                pool.wait_ge(br_out, 8 * (f // 4) + 4 + f % 4 + 1)
                pool.tensor_tensor(gates[:, f, :], gates[:, f, :], gates[:, 8 + f, :], ALU.add).then_inc(mg_sum, 1)
            for m in range(TB):
                rows_rsqrt(TB + m)
            for c in range(FF // P):
                pool.wait_ge(f1_hi, c + 1)
                pool.tensor_tensor(a_lo[:, c % KD, :], ff_sq[c % 2], a_hi[:, c % KD, :].bitcast(F32),
                                   ALU.subtract).then_inc(f1_cut, 1)

        @block.scalar
        def _(act):
            A = nc.scalar.activation

            def norm_square(m, src, junk):
                A(junk, src, ACT.Square, accum_out=row_ss[:, m:m + 1]).then_inc(row_sq, 1)

            def norm_hi(u, dst):
                m, hf = divmod(u % 8, 2)
                act.wait_ge(nt_gained, u + 1)
                A(dst[:, 4 * hf:4 * hf + 4, m * P:(m + 1) * P],
                  rows_t(u).rearrange("p (a b) -> p a b", a=4), ACT.Copy).then_inc(nt_hi, 1)

            nc.scalar.preload_act_table_set("natural_log_exp_and_others")
            for m in range(TB):
                act.wait_ge(x_in[m], 16)
                if m >= 1:
                    act.wait_ge(row_sq, m)
                norm_square(m, x_tok[:, m, :], slot(SQ, 2))
                if m == 0:
                    act.wait_ge(gain_t, 1)
                    A(gain[:, :], bank(7, 0, 20), ACT.Copy).then_inc(gain_ready, 1)
                    norm_hi(0, a_hi)
                    norm_hi(1, a_hi)
                else:
                    if m < 3:
                        act_cut(m - 1)
                    if m > 1:
                        norm_hi(2 * m - 2, a_hi)
                        norm_hi(2 * m - 1, a_hi)
            norm_hi(6, a_hi)
            norm_hi(7, a_hi)
            for j in (16, 18):
                A(gain[:, j:j + 1], gain[:, j:j + 1], ACT.Copy, scale=HD ** -0.5).then_inc(gain_ready, 1)
            act.wait_ge(kw_in, 16)
            A(kw_hi, kw_raw, ACT.Copy).then_inc(kw_hi_done, 1)

            def square(n):
                g, m = divmod(n, TB)
                act.wait_ge(proj_done, n + 1)
                if n >= 1:
                    act.wait_ge(ss_done, n)
                w = P if g == KVI else S
                A(slot(2)[:, 0:w], bank(m, 0, w), ACT.Square).then_inc(sq_done, 1)

            def turned(n):
                g, m = divmod(n, TB)
                act.wait_ge(tr_done, n + 1)
                b, t = 4 + n % 2, slice(m * P, (m + 1) * P)
                if g == KVI:
                    for q in range(2):
                        p = slice(64 * q, 64 * q + 64)
                        A(kz_sa[p, q, t], bank(b, 0, P)[p, :], ACT.Copy, scale=gain[p, 19:20])
                    A(q_parts[0][:, :, t], bank(b, P, 3 * P).rearrange("p (a b) -> p a b", a=2),
                      ACT.Copy).then_inc(qix_hi, 1)
                elif g == QSB:
                    for q in range(2):
                        p = slice(64 * q, 64 * q + 64)
                        ins = A(qz_sb[p, q::2, t], bank(b)[p, :].rearrange("p (a b) -> p a b", a=4), ACT.Copy,
                                scale=gain[p, 16:17])
                    ins.then_inc(tr_out, 1)
                else:
                    dst, gj = {KSB: (kT_sb, 17), QSA: (qT_sa, 18)}[g]
                    A(dst[:, :, t], bank(b).rearrange("p (a b) -> p a b", a=4), ACT.Copy,
                      scale=gain[:, gj:gj + 1]).then_inc(tr_out, 1)

            def index_start():
                act.wait_ge(wT_done, 1)
                A(w_tok[:, :, :], bank(7, 0, TB * IXH).rearrange("p (a b) -> p a b", a=TB), ACT.Copy,
                  scale=IXH ** -0.5).then_inc(w_ready, 1)
                act.wait_ge(ix_stacked, 20 * 16)
                A(q_stack[:, 0:4, :], q_in[:, 0:4, :], ACT.Copy).then_inc(ix_ready, 1)

            def index_relus(part):
                for u in range(4 * part, 4 * part + 4):
                    w = (u // 8 + 2) * P
                    act.wait_ge(rel_done, u + 1)
                    if u >= 2:
                        act.wait_ge(score_done, u - 1)
                    A(rel[u % 2][:, 0:w], bank(6 + u % 2, 0, w), ACT.Relu, scale=IXD ** -0.5).then_inc(relu_done, 1)

            for g in range(5):
                if g == KVI:
                    for m in range(3):
                        square(m)
                else:
                    if g == QSB:
                        act.wait_ge(gain_ready, 3)
                        act.wait_ge(q_zero, 1)
                    if g == KSB:
                        act.wait_ge(q_zero, 2)
                    for m in range(TB):
                        if g == KSB and m >= 2:
                            index_relus(m - 2)
                        turned(4 * (g - 1) + m)
                if g != KSB:
                    act_cut(2 * g + 2)
                if g < 4:
                    for m in range(3 if g == KVI else 0, TB):
                        if g == KSB:
                            index_relus(2 + m)
                        square(4 * g + m)
                        if g == KSB and m == 1:
                            act_cut(2 * g + 2)
                if g == QSB:
                    index_start()
                act_cut(2 * g + 3)

            def zset(h):
                return ps[:, 3 * (h % 2) * S:3 * (h % 2) * S + ZW]

            def log_part(h):
                act.wait_ge(z_done, h + 1)
                if h >= 2:
                    act.wait_ge(tri_done, h - 1)
                buf = lg[:, h % 2, :]
                A(buf, zset(h), ACT.Abs).then_inc(act_self, 1)
                act.wait_ge(act_self, 2 * h + 1)
                A(buf, buf, ACT.Exp, scale=-1.0).then_inc(act_self, 1)
                act.wait_ge(act_self, 2 * h + 2)
                A(buf, buf, ACT.Ln, bias=1.0).then_inc(ln_done, 1)

            def gate_out(f):
                act.wait_ge(gate_done, f + 1)
                A(gates[:, f, :], bank(7), ACT.Exp, scale=-1.0).then_inc(gate_exp, 1)

            glns = [0]

            def gate_sigmoid(f):
                act.wait_ge(gate_exp, f + 1)
                A(gates[:, f, :], gates[:, f, :], ACT.Ln, bias=1.0).then_inc(gate_ln, 1)
                glns[0] += 1
                act.wait_ge(gate_ln, glns[0])
                A(gates[:, f, :], gates[:, f, :], ACT.Exp, scale=-1.0).then_inc(gsb_ready if f < 8 else gsa_ready, 1)

            log_part(0)
            for h in range(SBH):
                if h % 2 == 0 and h:
                    act_cut(SL_GATE + 1 + h // 2)
                if h < 7:
                    log_part(h + 1)
                act.wait_ge(tri_done, h + 1)
                if h >= 2:
                    act.wait_ge(av_done, h // 2)
                A(weights[h % 2], zset(h), ACT.Exp).then_inc(a_done, 1)
                gate_out(h)
            for n in range(32 + 2):
                if n < 32:
                    w, j = (n // 8 + 1) * P, n % 4
                    act.wait_ge(smax_done, n + 1)
                    A(sa_s[j][:, 0:w], sa_s[j][:, 0:w], ACT.Exp, bias=snmax[:, j:j + 1], scale=-1.0,
                      accum_out=sum_p[:, j:j + 1]).then_inc(p_done, 1)
                if n >= 2:
                    q = n - 2
                    b, u = q // 8, q // 4
                    act.wait_ge(pt_done, q + 1)
                    if q == 0:
                        act.wait_ge(av_done, 4)
                    if u >= 2:
                        act.wait_ge(pv_done, u - 1)
                    A(pT[u % 2][:, q % 2, 0:b + 1, q % 4 // 2, :],
                      bank(2 + q % 2, 0, (b + 1) * P).rearrange("p (a b) -> p a b", b=P), ACT.Copy).then_inc(pt_out, 1)
                    if q % 4 == 3 and q < 31:
                        gate_out(8 + q // 4)
                if n % 8 in (2, 4) and n < 32:
                    act_cut(SL_GATE + 5 + n // 8, n % 8 // 2 - 1, 2)
                if n % 4 == 1 and n < 32:
                    gate_sigmoid(n // 4)
                if n % 4 == 3 and n >= 7:
                    gate_sigmoid(7 + n // 4)
            act.wait_ge(pv_done, 8)
            act.wait_ge(pt_out, 32)
            act.wait_ge(osb_out, 4)
            for c in range(8):
                if c == 4:
                    act.wait_ge(osa_out, 8)
                A(b_hi[:, c, :], (oT_sb if c < 4 else qT_sa)[:, c % 4, :], ACT.Copy).then_inc(o_hi, 1)
            gate_out(15)
            gate_sigmoid(15)
            act_cut(SL_BR + 1)
            for q in range(4):
                if q < 4:
                    act_cut(SL_BR + 2 + q)
                if q % 2:
                    for j in range(4):
                        f = 4 * (q // 2) + j
                        act.wait_ge(mg_sum, f + 1)
                        A(a_hi[:, f, :], gates[:, f, :], ACT.Copy).then_inc(mg_hi, 1)
            act_cut(SL_OUT + 2)
            act_cut(SL_OUT + 3)
            act_cut(SL_FF)
            for m in range(TB + 1):
                if m < TB:
                    act.wait_ge(wo_out, 4 + m + 1)
                    act.wait_ge(row_sq, TB + m)
                    norm_square(TB + m, xres[:, m, :], slot(14, 2))
                if m >= 1:
                    norm_hi(8 + 2 * (m - 1), b_hi)
                    norm_hi(9 + 2 * (m - 1), b_hi)
            act_cut(SL_FF + 1)

            def ff1_hidden(c):
                act.wait_ge(f1_done, c + 1)
                A(ff_relu[c % 2], bank(6 + c % 2), ACT.Relu).then_inc(f1_relu, 1)
                act.wait_ge(f1_sq, c + 1)
                A(a_hi[:, c % KD, :], ff_sq[c % 2], ACT.Copy).then_inc(f1_hi, 1)

            for g in range(FG):
                for j in range(8):
                    i = SL_FF + 8 * g + j
                    if j < 4:
                        ff1_hidden(8 * g + 2 * j)
                        ff1_hidden(8 * g + 2 * j + 1)
                    if i + 2 < SL_END:
                        act_cut(i + 2)

        @block.vector
        def _(dve):
            count = [0]

            def link(ins):
                count[0] += 1
                ins.then_inc(dve_self, 1)
                dve.wait_ge(dve_self, count[0])

            V = nc.vector

            dve.wait_ge(ident_done, 1)
            dve.wait_ge(const_made, 1)
            V.memset(cold_b[:, :], 0.0)
            V.tensor_copy(const_r[:, :, :], const_f[:, 0:2, :])
            V.tensor_copy(ident_b, ident[:, :])
            V.tensor_copy(mask_b, mask_f).then_inc(const_cut, 1)

            def norm_scale(m, dst, src):
                dve.wait_ge(row_ready, m + 1)
                V.tensor_scalar(dst, src, row_r[:, m:m + 1], None, ALU.mult).then_inc(row_scaled, 1)

            def norm_gain(u, g0):
                hf = u % 2
                dve.wait_ge(nt_done, u + 1)
                if u >= 2:
                    dve.wait_ge(nt_cut, u - 1)
                V.tensor_tensor(rows_t(u).rearrange("p (a b) -> p a b", a=4),
                                bank(4 + u % 2).rearrange("p (a b) -> p a b", a=4),
                                gain[:, g0 + 4 * hf:g0 + 4 * hf + 4].unsqueeze(2).to_broadcast([P, 4, P]),
                                ALU.mult).then_inc(nt_gained, 1)

            def norm_lo(u, hi, lo):
                m, hf = divmod(u % 8, 2)
                at = (slice(None), slice(4 * hf, 4 * hf + 4), slice(m * P, (m + 1) * P))
                dve.wait_ge(nt_hi, u + 1)
                V.tensor_tensor(lo[at], rows_t(u).rearrange("p (a b) -> p a b", a=4), hi[at].bitcast(F32),
                                ALU.subtract).then_inc(nt_cut, 1)

            def norm_block(m, g0, hi, lo):
                for u in (2 * m, 2 * m + 1):
                    norm_gain(u, g0)
                for u in (2 * m, 2 * m + 1):
                    norm_lo(u, hi, lo)

            norm_scale(0, x_tok[:, 0, :], x_tok[:, 0, :])
            dve.wait_ge(gain_ready, 1)
            norm_block(0, 0, a_hi, a_lo)
            for m in range(1, TB):
                norm_scale(m, x_tok[:, m, :], x_tok[:, m, :])
                if m < 3:
                    dve_cut(m - 1)
                if m >= 2:
                    norm_block(m - 1, 0, a_hi, a_lo)
            norm_block(3, 0, a_hi, a_lo)
            dve.wait_ge(kw_hi_done, 1)
            V.tensor_tensor(kw_lo, kw_raw, kw_hi.bitcast(F32), ALU.subtract).then_inc(kw_cut, 1)

            def topk_steps():
                for b in range(1, TB):
                    dve.wait_ge(causal_done, b)
                    for r in range(TOPK // 8):
                        link(V.max(best8[:, :], topmask[b]))
                        link(V.match_replace(out=topmask[b], in_to_replace=best8[:, :], in_values=topmask[b],
                                             imm_value=TAKEN))
                        yield
                    V.tensor_scalar(topmask[b], topmask[b], TAKEN * 0.5, MASKED, ALU.is_gt, ALU.mult).then_inc(mask_ready, 1)
                    yield

            steps = topk_steps()

            def topk(n):
                for _ in range(n):
                    next(steps, None)

            def head_sums(n):
                g, m = divmod(n, TB)
                nh = 2 if g == KVI else 8
                dve.wait_ge(sq_done, n + 1)
                if n >= 2:
                    dve.wait_ge(hr_done, n - 1)
                V.tensor_reduce(head_ss[:, n % 2, 0:nh], slot(2)[:, 0:nh * HD].rearrange("p (h d) -> p h d", d=HD),
                                AX.X, ALU.add).then_inc(ss_done, 1)

            def head_scaled(n):
                g, m = divmod(n, TB)
                nh = 2 if g == KVI else 8
                if n >= 2:
                    dve.wait_ge(tr_done, n - 1)
                dve.wait_ge(hr_done, n + 1)
                r = head_r[:, n % 2, 0:nh]
                if g == KVI:
                    V.tensor_copy(v_sa[:, m, :], bank(m, P, 2 * P))
                    V.tensor_copy(tok[n % 2][:, P:3 * P], bank(m, 2 * P, 4 * P))
                if g == QSA:
                    V.tensor_tensor(tok[n % 2].rearrange("p (r g d) -> p g r d", g=2, d=HD),
                                    bank(m).rearrange("p (g r d) -> p g r d", g=2, d=HD),
                                    r.rearrange("p (g r) -> p g r", g=2).unsqueeze(3).to_broadcast([P, 2, 4, HD]),
                                    ALU.mult).then_inc(proj_out, 1)
                else:
                    V.tensor_tensor(tok[n % 2][:, 0:nh * HD].rearrange("p (h d) -> p h d", d=HD),
                                    bank(m, 0, nh * HD).rearrange("p (h d) -> p h d", d=HD),
                                    r.unsqueeze(2).to_broadcast([P, nh, HD]), ALU.mult).then_inc(proj_out, 1)

            def index_scores(part):
                for u in range(4 * part, 4 * part + 4):
                    b, h = u // 8 + 1, u % 8
                    dve.wait_ge(relu_done, u + 1)
                    src, wgt = rel[u % 2][:, 0:(b + 1) * P], w_tok[:, b, h:h + 1]
                    if h == 0:
                        V.tensor_scalar(topmask[b], src, wgt, None, ALU.mult).then_inc(score_done, 1)
                    else:
                        dve.wait_ge(score_done, u)
                        V.scalar_tensor_tensor(out=topmask[b], in0=src, scalar=wgt, in1=topmask[b],
                                               op0=ALU.mult, op1=ALU.add).then_inc(score_done, 1)

            for g in range(5):
                if g == KVI:
                    head_sums(0)
                    head_scaled(0)
                    head_sums(1)
                    head_scaled(1)
                    head_sums(2)
                if g == QSB:
                    for m in range(TB):
                        dve.wait_ge(qix_hi, m + 1)
                        t = slice(m * P, (m + 1) * P)
                        V.tensor_tensor(q_parts[1][:, :, t], bank(4 + m % 2, P, 3 * P).rearrange("p (a b) -> p a b", a=2),
                                        q_parts[0][:, :, t].bitcast(F32), ALU.subtract).then_inc(tr_out, 1)
                if g == KSB:
                    dve.wait_ge(w_ready, 1)
                    index_scores(0)
                    index_scores(1)
                if g != KSB:
                    dve_cut(2 * g + 2)
                if g < 4:
                    if g == KVI:
                        dve.wait_ge(kix_done, 1)
                        link(V.tensor_copy(k_parts[0][0:IXD, :], bank(6)[0:IXD, :]))
                        V.tensor_tensor(k_parts[1][0:IXD, :], bank(6)[0:IXD, :], k_parts[0][0:IXD, :].bitcast(F32),
                                        ALU.subtract)
                        V.tensor_copy(kw_sb[32:40, :], bank(6)[32:40, :]).then_inc(kix_out, 1)
                    if g == KSB:
                        for m in range(TB):
                            index_scores(2 + m)
                            if m < 3:
                                head_sums(4 * g + m)
                            if m in (1, 2):
                                head_scaled(4 * g + m - 1)
                            if m == 1:
                                dve_cut(2 * g + 2)
                    for m in range(2 if g in (KVI, KSB) else 0, TB):
                        if g in (QSB, QSA) or m == 3:
                            head_sums(4 * g + m)
                        if g == QSB and m == 3:
                            dve.wait_ge(ix_stacked, 20 * 16)
                            V.tensor_copy(k_stack[:, :], k_in)
                            V.tensor_copy(q_stack[:, 4:8, :], q_in[:, 4:8, :]).then_inc(ix_ready, 1)
                        if g >= KSB:
                            topk(1)
                        head_scaled(4 * g + m)
                else:
                    for m in range(TB):
                        dve.wait_ge(proj_done, 16 + m + 1)
                        V.tensor_copy(v_sb[:, m, :], bank(m)).then_inc(proj_out, 1)
                        topk(1)
                dve_cut(2 * g + 3)
                if g in (KSB, QSA):
                    topk(4)

            def zset(h):
                return ps[:, 3 * (h % 2) * S:3 * (h % 2) * S + ZW]

            def softplus(h):
                buf = lg[:, h % 2, :]
                dve.wait_ge(ln_done, h + 1)
                link(V.scalar_tensor_tensor(out=buf, in0=zset(h), scalar=0.0, in1=buf, op0=ALU.max, op1=ALU.add))
                if h >= 1:
                    dve.wait_ge(tri_done, h)
                link(V.tensor_copy(sp_hi[:, :], buf))
                V.tensor_tensor(sp_lo[:, :], buf, sp_hi[:, :].bitcast(F32), ALU.subtract).then_inc(sp_done, 1)

            def sa_values_out(u):
                b, rp = divmod(u, 2)
                dve.wait_ge(pv_done, u + 1)
                V.tensor_copy(qT_sa[:, 2 * rp:2 * rp + 2, b * P:(b + 1) * P],
                              bank(4 + u % 2, 0, 2 * P).rearrange("p (a b) -> p a b", a=2)).then_inc(osa_out, 1)

            def sa_logits(n):
                w, j = (n // 8 + 1) * P, n % 4
                dve.wait_ge(s_done, n + 1)
                dve.wait_ge(bias_done, n + 1)
                dve.wait_ge(tri_done, 7 if n < 2 else 8)
                if n >= 4:
                    dve.wait_ge(pt_done, n - 3)
                V.tensor_tensor_reduce(out=sa_s[j][:, 0:w], in0=bank(n % 2, 0, w), in1=sa_bias[j][:, 0:w],
                                       scale=-1.0, scalar=3.0e38, op0=ALU.add, op1=ALU.min,
                                       accum_out=snmax[:, j:j + 1]).then_inc(smax_done, 1)

            def pair_out(c):
                dve.wait_ge(av_done, c + 1)
                V.tensor_copy(oT_sb[:, c, :], bank(6)).then_inc(osb_out, 1)

            for h in range(SBH):
                softplus(h)
                if h % 2 == 0 and h:
                    dve_cut(SL_GATE + 1 + h // 2)
                topk(2 if h == 0 else 3)
                if h % 2 == 0 and h:
                    pair_out(h // 2 - 1)
            sa_logits(0)
            sa_logits(1)
            for n in range(2, 32 + 2):
                if n == 4:
                    pair_out(3)
                if n < 32:
                    sa_logits(n)
                q = n - 2
                w, j = (q // 8 + 1) * P, q % 4
                dve.wait_ge(p_done, q + 1)
                link(V.reciprocal(rcp_l[:, j:j + 1], sum_p[:, j:j + 1]))
                V.tensor_scalar(sa_s[j][:, 0:w], sa_s[j][:, 0:w], rcp_l[:, j:j + 1], None, ALU.mult).then_inc(pn_done, 1)
                topk(0 if n < 8 else 1 if n < 20 else 60)
                if n % 8 in (5, 6) and n < 32:
                    dve_cut(SL_GATE + 5 + n // 8, n % 8 - 5, 2)
                if n >= 8 and n % 4 == 0:
                    sa_values_out(n // 4 - 2)
            sa_values_out(7)
            for c in range(8):
                dve.wait_ge(o_hi, c + 1)
                V.tensor_tensor(b_lo[:, c, :], (oT_sb if c < 4 else qT_sa)[:, c % 4, :],
                                b_hi[:, c, :].bitcast(F32), ALU.subtract).then_inc(o_cut, 1)
            dve_cut(SL_BR + 1)
            for q in range(4):
                dve_cut(SL_BR + 2 + q)
                dve.wait_ge(*((gsb_ready, 8) if q % 2 == 0 else (gsa_ready, 4 * (q // 2) + 4)))
                for j in range(4):
                    f = 8 * (q % 2) + 4 * (q // 2) + j
                    dve.wait_ge(br_done, 4 * q + j + 1)
                    V.tensor_tensor(gates[:, f, :], bank(4 * (q % 2) + j), gates[:, f, :], ALU.mult).then_inc(br_out, 1)
                if q % 2:
                    for j in range(4):
                        f = 4 * (q // 2) + j
                        dve.wait_ge(mg_hi, f + 1)
                        V.tensor_tensor(a_lo[:, f, :], gates[:, f, :], a_hi[:, f, :].bitcast(F32),
                                        ALU.subtract).then_inc(mg_cut, 1)
            def add_to_x(n, m):
                part = xres[:, m, n * 512:(n + 1) * 512]
                return V.tensor_tensor(part, bank(m), part, ALU.add)

            dve_cut(SL_OUT + 2)
            for m in range(TB):
                dve.wait_ge(x2_in[m], 16)
                dve.wait_ge(wo_done, m + 1)
                add_to_x(0, m).then_inc(wo_out, 1)
            dve_cut(SL_OUT + 3)
            dve_cut(SL_FF)
            for m in range(TB + 1):
                if m < TB:
                    dve.wait_ge(wo_done, 4 + m + 1)
                    add_to_x(1, m).then_inc(wo_out, 1)
                    norm_scale(TB + m, xn2[m % 2], xres[:, m, :])
                if m >= 1:
                    norm_block(TB + m - 1, 8, b_hi, b_lo)
            dve_cut(SL_FF + 1)

            def ff1_square(c):
                dve.wait_ge(f1_relu, c + 1)
                if c >= 2:
                    dve.wait_ge(f1_cut, c - 1)
                V.scalar_tensor_tensor(out=ff_sq[c % 2], in0=bank(6 + c % 2), scalar=0.0, in1=ff_relu[c % 2],
                                       op0=ALU.max, op1=ALU.mult).then_inc(f1_sq, 1)

            for g in range(FG):
                for j in range(8):
                    i = SL_FF + 8 * g + j
                    if j < 4:
                        ff1_square(8 * g + 2 * j)
                        ff1_square(8 * g + 2 * j + 1)
                    if j in (5, 7):
                        n = (j - 5) // 2
                        for m in range(TB):
                            dve.wait_ge(f2_done, 8 * g + 4 * n + m + 1)
                            add_to_x(n, m).then_inc(f2_out, 1)
                    if i + 2 < SL_END:
                        dve_cut(i + 2)

        @block.tensor
        def _(pe):
            T = nc.tensor

            def norm_turn(m, src):
                pe.wait_ge(row_scaled, m + 1)
                for hf in range(2):
                    u = 2 * m + hf
                    if u >= 2:
                        pe.wait_ge(nt_gained, u - 1)
                    for k in range(4):
                        t = T.transpose(bank(4 + u % 2, k * P, (k + 1) * P),
                                        src[:, (4 * hf + k) * P:(4 * hf + k + 1) * P], ident[:, :])
                    t.then_inc(nt_done, 1)

            def keep_warm(n):
                for _ in range(n):
                    T.matmul(bank(6), ident_b, cold_b[:, :], start=True, stop=True)

            pe.wait_ge(const_cut, 1)
            keep_warm(WARM[0])
            pe.wait_ge(ident_done, 1)
            pe.wait_ge(gains_in, 96)
            T.transpose(bank(7, 0, 20), gain_rows[:, :], ident[0:20, 0:20]).then_inc(gain_t, 1)

            def slab_ready(i):
                pe.wait_ge(lo_done, i + 1)

            def project_part(g, half, m, between=None):
                for k in range(4):
                    kk, t = 4 * half + k, slice(m * P, (m + 1) * P)
                    mm = moving_weights(SL_PROJ + 2 * g + half, k, bank(m), a_hi[:, kk, t], a_lo[:, kk, t],
                                        start=(kk == 0), stop=(kk == 7))
                    if between is not None:
                        between(k)
                return mm

            def project(g, half, index=False):
                slab_ready(SL_PROJ + 2 * g + half)
                for m in range(TB):
                    if half == 0:
                        pe.wait_ge(proj_out, 4 * (g - 1) + m + 1)
                    u0 = 4 * (4 * half + m - 2)
                    if index and u0 == 0:
                        pe.wait_ge(ix_ready, 2)
                        pe.wait_ge(w_ready, 1)
                    mm = project_part(g, half, m, (lambda k: index_logits(u0 + k)) if index and u0 >= 0 else None)
                    if half == 1:
                        mm.then_inc(proj_done, 1)
                    elif m == TB - 1:
                        mm.then_inc(half_done, 1)
                    if half == 0:
                        turn(4 * (g - 1) + m)

            def turn(n):
                g, m = divmod(n, TB)
                pe.wait_ge(proj_out, n + 1)
                if n >= 2:
                    pe.wait_ge(tr_out, n - 1)
                for k in range(3 if g == KVI else 4):
                    t = T.transpose(bank(4 + n % 2, k * P, (k + 1) * P), tok[n % 2][:, k * P:(k + 1) * P], ident[:, :])
                t.then_inc(tr_done, 1)

            norm_turn(0, x_tok[:, 0, :])
            keep_warm(WARM[1])
            norm_turn(1, x_tok[:, 1, :])
            for m in range(TB):
                pe.wait_ge(nt_cut, 2 * m + 2)
                if m == 0:
                    slab_ready(0)
                project_part(KVI, 0, m)
                if m == 0:
                    slab_ready(1)
                if m == 1:
                    norm_turn(2, x_tok[:, 2, :])
                project_part(KVI, 1, m).then_inc(proj_done, 1)
                if m == 1:
                    norm_turn(3, x_tok[:, 3, :])
            pe.wait_ge(kw_cut, 1)
            for k in range(KD):
                T.matmul(bank(6)[0:40, :], kw_hi[:, k, :], a_hi[:, k, :], start=(k == 0), stop=False)
                T.matmul(bank(6)[0:40, :], kw_hi[:, k, :], a_lo[:, k, :], start=False, stop=False)
                mm = T.matmul(bank(6)[0:40, :], kw_lo[:, k, :], a_hi[:, k, :], start=False, stop=(k == KD - 1))
            mm.then_inc(kix_done, 1)

            def index_weights():
                pe.wait_ge(kix_out, 1)
                for m in range(TB):
                    t = T.transpose(bank(7, m * IXH, (m + 1) * IXH), kw_sb[32:40, m * P:(m + 1) * P], ident[32:40, 32:40])
                t.then_inc(wT_done, 1)

            def index_logits(u):
                b, h = u // 8 + 1, u % 8
                if u >= 2:
                    pe.wait_ge(relu_done, u - 1)
                T.matmul(bank(6 + u % 2, 0, (b + 1) * P), q_stack[:, h, b * P:(b + 1) * P],
                         k_stack[:, 0:(b + 1) * P], start=True, stop=True).then_inc(rel_done, 1)

            for g in range(1, 5):
                if g == KSB:
                    index_weights()
                project(g, 0, g == KSB)
                project(g, 1, g == KSB)

            def zt(h, i, t0=None):
                t0 = i if t0 is None else t0
                a = 3 * (h % 2) * S + ZCOL[i]
                return ps[:, a + (t0 - i) * P:a + (4 - i) * P]

            def logits(h):
                c = h // 2
                if h >= 2:
                    pe.wait_ge(a_done, h - 1)
                for i in range(4):
                    T.matmul(zt(h, i), kT_sb[:, c, i * P:(i + 1) * P], qz_sb[:, h, i * P:S],
                             start=(i != 3), stop=False, skip_group_check=True)
                    mm = T.matmul(zt(h, i)[:, 0:P], ident_b, mask_b, start=False, stop=False, skip_group_check=True)
                mm.then_inc(z_done, 1)

            def sum_later(h):
                pe.wait_ge(sp_done, h + 1)
                for i in range(4):
                    for j in range(i, 4):
                        a = ZCOL[j]
                        if j == 3:
                            mm = T.matmul(zt(h, i, j), tri_f if i == j else ones_f, lg[:, h % 2, a:a + P],
                                          start=False, stop=True, skip_group_check=True)
                            continue
                        for part in (sp_hi, sp_lo):
                            mm = T.matmul(zt(h, i, j), tri_r if i == j else ones_r, part[:, a:a + (4 - j) * P],
                                          start=False, stop=False, skip_group_check=True)
                mm.then_inc(tri_done, 1)

            def weighted_values(c):
                pe.wait_ge(a_done, 2 * c + 2)
                if c >= 1:
                    pe.wait_ge(osb_out, c)
                for i in range(4):
                    for h in (2 * c, 2 * c + 1):
                        p0 = 64 * (h % 2)
                        mm = T.matmul(bank(6, i * P, S)[p0:p0 + 64, :], v_sb[:, i, h * HD:(h + 1) * HD],
                                      weights[h % 2][:, ZCOL[i]:ZCOL[i] + (4 - i) * P], start=(i == 0), stop=(i == 3),
                                      skip_group_check=True)
                mm.then_inc(av_done, 1)

            def gate(f, k0=0, k1=KD):
                i = SL_GATE + f // 2
                if k0 == 0:
                    slab_ready(i)
                    if f >= 1:
                        pe.wait_ge(gate_exp, f)
                for k in range(k0, k1):
                    mm = stationary_weights(i, k, KD, (f % 2) * P, bank(7), a_hi[:, k, :], a_lo[:, k, :],
                                            start=(k == 0), stop=(k == KD - 1))
                if k1 == KD:
                    mm.then_inc(gate_done, 1)

            def sa_scores(n):
                b = n // 8
                r, g = divmod(n % 8, SAKV)
                if n >= 2:
                    pe.wait_ge(smax_done, n - 1)
                T.matmul(bank(n % 2, 0, (b + 1) * P), qT_sa[:, r, b * P:(b + 1) * P],
                         kz_sa[:, g, 0:(b + 1) * P], start=True, stop=True).then_inc(s_done, 1)

            pe.wait_ge(const_cut, 1)
            pe.wait_ge(tr_out, 16)
            pe.wait_ge(proj_out, 19)
            pe.wait_ge(score_done, 24)
            logits(0)
            for h in range(SBH):
                if h == 0:
                    pe.wait_ge(proj_out, 20)
                if h < 7:
                    logits(h + 1)
                gate(h, 0, 4 if h else 8)
                if h == 7:
                    sa_scores(0)
                    sa_scores(1)
                sum_later(h)
                if h:
                    gate(h, 4, 8)
                if h % 2:
                    weighted_values(h // 2)

            def sa_turn(n):
                b = n // 8
                pe.wait_ge(pn_done, n + 1)
                if n >= 2:
                    pe.wait_ge(pt_out, n - 1)
                for i in range(b + 1):
                    t = T.transpose(bank(2 + n % 2, i * P, (i + 1) * P), sa_s[n % 4][:, i * P:(i + 1) * P], ident[:, :])
                t.then_inc(pt_done, 1)

            def sa_values(u):
                b = u // 2
                pe.wait_ge(pt_out, 4 * u + 4)
                if u >= 2:
                    pe.wait_ge(osa_out, u - 1)
                for i in range(b + 1):
                    for g in range(SAKV):
                        mm = T.matmul(bank(4 + u % 2, 0, 2 * P)[64 * g:64 * g + 64, :], v_sa[:, i, 64 * g:64 * g + 64],
                                      pT[u % 2][:, g, i], start=(i == 0), stop=(i == b))
                mm.then_inc(pv_done, 1)

            pe.wait_ge(a_done, 8)
            sa_scores(2)
            for n in range(32):
                sa_turn(n)
                if n < 29:
                    sa_scores(n + 3)
                if n < 28:
                    gate(8 + n // 4, 2 * (n % 4), 2 * (n % 4) + 2)
                if n >= 4 and n % 4 == 0:
                    sa_values(n // 4 - 1)
            gate(15, 0, 4)
            sa_values(7)
            gate(15, 4, 8)

            pe.wait_ge(osa_out, 8)
            for q in range(4):
                i = SL_BR + q
                slab_ready(i)
                for j in range(4):
                    if q == 1 and j == 3:
                        pe.wait_ge(gate_exp, 16)
                    if q >= 2:
                        pe.wait_ge(br_out, 4 * (q - 2) + j + 1)
                    for k in range(4):
                        c = 4 * (q % 2) + k
                        if q < 2 and j == 0:
                            pe.wait_ge(o_cut, c + 1)
                        mm = stationary_weights(i, k, 4, j * P, bank(4 * (q % 2) + j), b_hi[:, c, :], b_lo[:, c, :],
                                                start=(k == 0), stop=(k == 3))
                    mm.then_inc(br_done, 1)

            def out_part(n, half, m):
                for k in range(4):
                    kk, t = 4 * half + k, slice(m * P, (m + 1) * P)
                    if n == 0 and m == 0:
                        pe.wait_ge(mg_cut, kk + 1)
                    mm = moving_weights(SL_OUT + 2 * n + half, k, bank(m), a_hi[:, kk, t], a_lo[:, kk, t],
                                        start=(kk == 0), stop=(kk == 7))
                return mm

            slab_ready(SL_OUT)
            pe.wait_ge(br_out, 12)
            for m in range(TB):
                mm = out_part(0, 0, m)
            mm.then_inc(half_done, 1)
            slab_ready(SL_OUT + 1)
            for m in range(TB):
                out_part(0, 1, m).then_inc(wo_done, 1)
            for m in range(2):
                pe.wait_ge(wo_out, m + 1)
                out_part(1, 0, m)
            slab_ready(SL_OUT + 3)
            for m in range(TB):
                if m >= 2:
                    pe.wait_ge(wo_out, m + 1)
                    out_part(1, 0, m)
                out_part(1, 1, m).then_inc(wo_done, 1)
                if m >= 1:
                    norm_turn(TB + m - 1, xn2[(m - 1) % 2])

            def ff1_part(c, t0, t1):
                for k in range(KD):
                    mm = stationary_weights(SL_FF + 8 * (c // 8) + c % 8 // 2, k, KD, (c % 2) * P,
                                            bank(6 + c % 2, t0, t1), b_hi[:, k, t0:t1], b_lo[:, k, t0:t1],
                                            start=(k == 0), stop=(k == KD - 1))
                return mm

            slab_ready(SL_FF)
            pe.wait_ge(nt_cut, 12)
            ff1_part(0, 0, 256)
            norm_turn(TB + 3, xn2[1])
            ff1_part(1, 0, 256)

            pe.wait_ge(nt_cut, 16)
            for g in range(FG):
                for j in range(4):
                    i = SL_FF + 8 * g + j
                    slab_ready(i)
                    for o in range(2):
                        c = 8 * g + 2 * j + o
                        if c >= 2:
                            pe.wait_ge(f1_sq, c - 1)
                        ff1_part(c, 0 if c >= 2 else 256, S).then_inc(f1_done, 1)
                for q in range(4):
                    n, half = divmod(q, 2)
                    i = SL_FF + 8 * g + 4 + q
                    slab_ready(i)
                    for m in range(TB):
                        e = 8 * g + 4 * n + m
                        if half == 0:
                            if e >= 4:
                                pe.wait_ge(f2_out, e - 3)
                            else:
                                pe.wait_ge(wo_out, 5 + m)
                        for k in range(4):
                            kk, t = 4 * half + k, slice(m * P, (m + 1) * P)
                            if n == 0 and m == 0:
                                pe.wait_ge(f1_cut, 8 * g + kk + 1)
                            mm = moving_weights(i, k, bank(m), a_hi[:, kk, t], a_lo[:, kk, t],
                                                start=(kk == 0), stop=(kk == 7))
                        if half == 1:
                            mm.then_inc(f2_done, 1)
                    if half == 0:
                        mm.then_inc(half_done, 1)


_INS = ["x", "norm_mix", "w_in", "q_norm_sb", "k_norm_sb", "q_norm_sa", "k_norm_sa",
        "w_branch_sb", "w_branch_sa", "w_out", "norm_mlp", "w_ff1", "w_ff2"]
_OUTS = [((1, S, D), "float32")]


def kernel(**inputs):
    import numpy as _np
    import concourse.bacc as _bacc
    from concourse import mybir as _mybir
    from concourse.bass_utils import run_bass_kernel_spmd as _run

    nc = _bacc.Bacc("TRN2", target_bir_lowering=False, num_devices=1)
    arrays, args = {}, []
    for name in _INS:
        a = _np.ascontiguousarray(inputs[name])
        arrays[f"in_{name}_dram"] = a
        args.append(nc.dram_tensor(f"in_{name}_dram", a.shape, _mybir.dt.from_np(a.dtype), kind="ExternalInput").ap())
    for i, (shape, dtype) in enumerate(_OUTS):
        dt = _mybir.dt.from_np(_np.dtype(dtype))
        args.append(nc.dram_tensor(f"out_{i}_dram", shape, dt, kind="ExternalOutput").ap())
    block_kernel(nc, *args)
    r = _run(nc, [arrays], core_ids=[0])
    got = tuple(r.results[0][f"out_{i}_dram"] for i in range(len(_OUTS)))
    return got[0]
```
